# Optimizing a Trainium2 kernel written in Bass

```python
import jax, jax.numpy as jnp
from jax import lax
import numpy as np

D_MODEL = 2048
BATCH = 1
SEQ = 256
DEPTH = 2

N_MIXERS = 2
HEAD_DIM = 128
N_QK_HEADS = D_MODEL // HEAD_DIM
N_V_HEADS = 2 * N_QK_HEADS
QK_DIM = N_QK_HEADS * HEAD_DIM
V_DIM = N_V_HEADS * HEAD_DIM
GDN_CONV_DIM = 2 * QK_DIM + V_DIM
GDN_PROJ_DIM = GDN_CONV_DIM + V_DIM + 4 * N_V_HEADS
SHORT_CONV_WIDTH = 5
CHUNK = 64
CONF_WIDTH = 31
FFN_HIDDEN = (8 * D_MODEL + 3 * 256 - 1) // (3 * 256) * 256
N_GDN_LAYERS = (DEPTH + 1) // 2
N_CONF_LAYERS = DEPTH // 2
RMS_EPS = 1e-6
LN_EPS = 1e-5
L2_EPS = 1e-6

kernel_name = "hybrid_gdn_conformer_encoder"

def rmsnorm(x, w):
    xf = x.astype(jnp.float32)
    y = xf * lax.rsqrt(jnp.mean(xf * xf, axis=-1, keepdims=True) + RMS_EPS)
    return (y * w.astype(jnp.float32)).astype(x.dtype)

def layernorm(x, w, b):
    xf = x.astype(jnp.float32)
    mu = jnp.mean(xf, axis=-1, keepdims=True)
    xc = xf - mu
    y = xc * lax.rsqrt(jnp.mean(xc * xc, axis=-1, keepdims=True) + LN_EPS)
    return (y * w.astype(jnp.float32) + b.astype(jnp.float32)).astype(x.dtype)

def l2norm(x):
    return x * lax.rsqrt(jnp.sum(x * x, axis=-1, keepdims=True) + L2_EPS)

def depthwise_conv(x, w):
    K = w.shape[0]
    return lax.conv_general_dilated(
        x, w[:, None, :].astype(x.dtype), window_strides=(1,),
        padding=[(K // 2, K - 1 - K // 2)],
        dimension_numbers=('NWC', 'WIO', 'NWC'),
        feature_group_count=x.shape[-1])

def chunk_gated_delta_rule(q, k, v, g, beta):
    B, T, H, DK = q.shape
    DV = v.shape[-1]
    N = T // CHUNK

    def chunks(t):
        t = t.reshape((B, N, CHUNK, H) + t.shape[3:])
        return t.transpose((1, 0, 3, 2) + tuple(range(4, t.ndim)))

    q = chunks(q) * (DK ** -0.5)
    k = chunks(k)
    v = chunks(v)
    beta = chunks(beta)
    g = jnp.cumsum(chunks(g), axis=-1)
    idx = jnp.arange(CHUNK)
    incl = idx[:, None] >= idx[None, :]
    strict = idx[:, None] > idx[None, :]
    decay = jnp.exp(jnp.where(incl, g[..., :, None] - g[..., None, :], -jnp.inf))
    k_beta = k * beta[..., None]
    lower = jnp.where(strict, jnp.einsum('nbhid,nbhjd->nbhij', k_beta, k) * decay, 0.0)
    eye = jnp.eye(CHUNK, dtype=lower.dtype)
    rhs = jnp.concatenate([v * beta[..., None], k_beta * jnp.exp(g)[..., None]], axis=-1)
    sol = lax.linalg.triangular_solve(eye + lower, rhs, left_side=True, lower=True)
    u, w = sol[..., :DV], sol[..., DV:]
    a_qk = jnp.einsum('nbhid,nbhjd->nbhij', q, k) * decay
    q_g = q * jnp.exp(g)[..., None]
    g_last = g[..., -1:]
    k_tail = k * jnp.exp(g_last - g)[..., None]
    chunk_decay = jnp.exp(g_last)[..., None]

    def step(S, xs):
        u_i, w_i, a_i, qg_i, kt_i, cd_i = xs
        v_new = u_i - jnp.einsum('bhcd,bhde->bhce', w_i, S)
        o_i = jnp.einsum('bhcd,bhde->bhce', qg_i, S) + jnp.einsum('bhij,bhje->bhie', a_i, v_new)
        S = S * cd_i + jnp.einsum('bhcd,bhce->bhde', kt_i, v_new)
        return S, o_i

    S0 = jnp.zeros((B, H, DK, DV), jnp.float32)
    _, o = lax.scan(step, S0, (u, w, a_qk, q_g, k_tail, chunk_decay))
    return o.transpose(1, 0, 3, 2, 4).reshape(B, T, H, DV)

def gated_deltanet(h, in_w, conv_w, A_log, dt_bias, norm_w, out_w):
    B, T, _ = h.shape
    proj = h @ in_w
    qkv = proj[..., :GDN_CONV_DIM]
    z = proj[..., GDN_CONV_DIM:GDN_CONV_DIM + V_DIM]
    ba = proj[..., GDN_CONV_DIM + V_DIM:].astype(jnp.float32).reshape(B, T, 2, 2, N_V_HEADS)
    qkv = jax.nn.silu(depthwise_conv(qkv, conv_w)).astype(jnp.float32)
    q = qkv[..., :QK_DIM].reshape(B, T, N_QK_HEADS, HEAD_DIM)
    k = qkv[..., QK_DIM:2 * QK_DIM].reshape(B, T, N_QK_HEADS, HEAD_DIM)
    v = qkv[..., 2 * QK_DIM:].reshape(B, T, N_V_HEADS, HEAD_DIM)
    rep = N_V_HEADS // N_QK_HEADS
    q = jnp.repeat(l2norm(q), rep, axis=2)
    k = jnp.repeat(l2norm(k), rep, axis=2)
    beta = jax.nn.sigmoid(ba[:, :, 0])
    g = -jnp.exp(A_log.astype(jnp.float32)) * jax.nn.softplus(ba[:, :, 1] + dt_bias.astype(jnp.float32))
    o_f = chunk_gated_delta_rule(q, k, v, g[:, :, 0], beta[:, :, 0])
    flip = lambda t: jnp.flip(t, axis=1)
    o_b = flip(chunk_gated_delta_rule(flip(q), flip(k), flip(v), flip(g[:, :, 1]), flip(beta[:, :, 1])))
    o = o_f + o_b
    o = rmsnorm(o, norm_w) * jax.nn.silu(z.astype(jnp.float32).reshape(B, T, N_V_HEADS, HEAD_DIM))
    return o.reshape(B, T, V_DIM).astype(h.dtype) @ out_w

def conformer_conv(h, pw1_w, pw1_b, dw_w, dw_b, ln_w, ln_b, pw2_w, pw2_b):
    u = h @ pw1_w + pw1_b
    a, gate = jnp.split(u, 2, axis=-1)
    u = a * jax.nn.sigmoid(gate)
    u = depthwise_conv(u, dw_w) + dw_b
    u = jax.nn.silu(layernorm(u, ln_w, ln_b))
    return u @ pw2_w + pw2_b

def swiglu(h, in_w, out_w):
    gu = h @ in_w
    gate, up = jnp.split(gu, 2, axis=-1)
    return (jax.nn.silu(gate) * up) @ out_w

def setup_inputs(seed: int = 0) -> dict:
    key = jax.random.key(seed)
    ks = iter(jax.random.split(key, 32))
    f32 = jnp.float32
    nrm = lambda shape, s: jax.random.normal(next(ks), shape, f32) * s
    D = D_MODEL
    dt = jnp.exp(jax.random.uniform(next(ks), (N_GDN_LAYERS, 2, N_V_HEADS), f32,
                                    float(np.log(1e-3)), float(np.log(1e-1))))
    return {
        "x": nrm((BATCH, SEQ, D), 1.0),
        "c": nrm((BATCH, D), 1.0),
        "ada_w": nrm((DEPTH, D, 6 * D), 0.5 * D ** -0.5),
        "ada_b": nrm((DEPTH, 6 * D), 0.02),
        "norm_w": 1.0 + nrm((DEPTH, 4, D), 0.1),
        "gdn_in_w": nrm((N_GDN_LAYERS, D, GDN_PROJ_DIM), D ** -0.5),
        "gdn_conv_w": nrm((N_GDN_LAYERS, SHORT_CONV_WIDTH, GDN_CONV_DIM), SHORT_CONV_WIDTH ** -0.5),
        "gdn_A_log": jnp.log(jax.random.uniform(next(ks), (N_GDN_LAYERS, 2, N_V_HEADS), f32, 1.0, 16.0)),
        "gdn_dt_bias": dt + jnp.log(-jnp.expm1(-dt)),
        "gdn_norm_w": 1.0 + nrm((N_GDN_LAYERS, HEAD_DIM), 0.1),
        "gdn_out_w": nrm((N_GDN_LAYERS, V_DIM, D), V_DIM ** -0.5),
        "cf_pw1_w": nrm((N_CONF_LAYERS, D, 2 * D), D ** -0.5),
        "cf_pw1_b": nrm((N_CONF_LAYERS, 2 * D), 0.02),
        "cf_dw_w": nrm((N_CONF_LAYERS, CONF_WIDTH, D), CONF_WIDTH ** -0.5),
        "cf_dw_b": nrm((N_CONF_LAYERS, D), 0.02),
        "cf_ln_w": 1.0 + nrm((N_CONF_LAYERS, D), 0.1),
        "cf_ln_b": nrm((N_CONF_LAYERS, D), 0.02),
        "cf_pw2_w": nrm((N_CONF_LAYERS, D, D), D ** -0.5),
        "cf_pw2_b": nrm((N_CONF_LAYERS, D), 0.02),
        "ffn_in_w": nrm((DEPTH, D, 2 * FFN_HIDDEN), D ** -0.5),
        "ffn_out_w": nrm((DEPTH, FFN_HIDDEN, D), FFN_HIDDEN ** -0.5),
    }

def reference(x, c, ada_w, ada_b, norm_w, gdn_in_w, gdn_conv_w, gdn_A_log, gdn_dt_bias,
              gdn_norm_w, gdn_out_w, cf_pw1_w, cf_pw1_b, cf_dw_w, cf_dw_b, cf_ln_w, cf_ln_b,
              cf_pw2_w, cf_pw2_b, ffn_in_w, ffn_out_w):
    cond = jax.nn.silu(c)
    for i in range(DEPTH):
        mod = (cond @ ada_w[i] + ada_b[i])[:, None, :]
        sh1, sc1, g1, sh2, sc2, g2 = jnp.split(mod, 6, axis=-1)
        h = rmsnorm(x, norm_w[i, 0]) * (1 + sc1) + sh1
        j = i // N_MIXERS
        if i % N_MIXERS == 0:
            h = gated_deltanet(h, gdn_in_w[j], gdn_conv_w[j], gdn_A_log[j], gdn_dt_bias[j],
                               gdn_norm_w[j], gdn_out_w[j])
        else:
            h = conformer_conv(h, cf_pw1_w[j], cf_pw1_b[j], cf_dw_w[j], cf_dw_b[j],
                               cf_ln_w[j], cf_ln_b[j], cf_pw2_w[j], cf_pw2_b[j])
        x = x + (1 + g1) * rmsnorm(h, norm_w[i, 1])
        h = rmsnorm(x, norm_w[i, 2]) * (1 + sc2) + sh2
        h = swiglu(h, ffn_in_w[i], ffn_out_w[i])
        x = x + (1 + g2) * rmsnorm(h, norm_w[i, 3])
    return x


_drawn_inputs = setup_inputs


def setup_inputs(seed=0):
    import zlib

    import numpy as np

    out = dict(_drawn_inputs(seed))
    spreads = {}
    factors = {'cf_pw1_b': 5.313, 'cf_dw_b': 3.037, 'cf_ln_b': 5.366, 'cf_pw2_b': 3.136}
    for name, (base, spread) in spreads.items():
        noise = np.random.default_rng([zlib.crc32(name.encode()), seed]).standard_normal(out[name].shape)
        drawn = base * np.exp(spread * noise) if base else spread * noise
        out[name] = __import__('jax').numpy.asarray(drawn.astype(out[name].dtype))
    for name, factor in factors.items():
        out[name] = (out[name] * factor).astype(out[name].dtype)
    return out
```

```python
import concourse.bass as bass
from concourse import mybir
from contextlib import ExitStack, contextmanager

P = 128
D = 2048
T = 256
TT = T // P
KC = D // P
NSL = 512
KT = 4
TILE = KT * NSL
HQ, HV = 16, 32
QKV = 2 * HQ * P + HV * P
NQKV = QKV // NSL
VD = HV * P
NZ = VD // NSL
TAPS = 5
CTAPS = 31
HID = 5632
GRP = HID // NSL
NBLK = T // 32
RMS_EPS, LN_EPS, L2_EPS = 1e-6, 1e-5, 1e-6


class Tally:

    def __init__(self, sem, n=0):
        self.sem, self.n, self.off = sem, n, 0

    def inc(self, instruction):
        instruction.then_inc(self.sem, 1)
        self.n += 1

    def at(self):
        return self.n + self.off

    def wait(self, engine):
        engine.wait_ge(self.sem, self.at())

    @contextmanager
    def loop(self, engine, start, end, per):
        n0 = self.n
        with engine.Fori(start, end) as i:
            self.off = (i - start) * per
            yield i
        assert self.n == n0 + per
        self.n, self.off = n0 + per * (end - start), 0


def build(nc, x_in, c_in, ada_w, ada_b, norm_w, gdn_in_w, gdn_conv_w, gdn_A_log, gdn_dt_bias,
          gdn_norm_w, gdn_out_w, cf_pw1_w, cf_pw1_b, cf_dw_w, cf_dw_b, cf_ln_w, cf_ln_b,
          cf_pw2_w, cf_pw2_b, ffn_in_w, ffn_out_w, out):
    F32, F32R = mybir.dt.float32, mybir.dt.float32r
    ALU = mybir.AluOpType
    ACT = mybir.ActivationFunctionType
    AX = mybir.AxisListType.X
    ds = bass.ds
    MUL, ADD, SUB, MIN = ALU.mult, ALU.add, ALU.subtract, ALU.min

    G_BA = 0
    G_QKV = 1
    G_Z = G_QKV + 4 * NQKV
    G_GO = G_Z + 4 * NZ
    G_F0 = G_GO + 8 * 4
    G_P1 = G_F0 + 12 * GRP
    G_P2 = G_P1 + 4 * 8
    G_F1 = G_P2 + 4 * 4
    S_BA = 0
    S_QKV = 1
    S_Z = S_QKV + NQKV
    S_GO = S_Z + NZ
    S_F0 = S_GO + 4
    S_P1 = S_F0 + 6 * GRP
    S_P2 = S_P1 + 8
    S_F1 = S_P2 + 4
    MODS = [0, 1, 2, 3, 4]

    stack = ExitStack()
    with stack:
        def sb(name, shape, dt=F32, at=stack):
            return at.enter_context(nc.sbuf_tensor(name, shape, dt))

        def sem(name):
            return stack.enter_context(nc.semaphore(name))

        def dram(name, shape):
            return nc.dram_tensor(name, shape, F32, kind="Internal").ap()

        d_qkn = dram("d_qkn", (2 * HQ, P, T))
        d_v = dram("d_v", (TT, P, VD))
        d_z = dram("d_z", (TT, P, VD))
        d_rows = dram("d_rows", (8 * HQ, T))
        d_kk = dram("d_kk", (HQ * NBLK, 32, 32))
        d_inv = dram("d_inv", (HQ * NBLK, 2, 4, 32, 32))
        d_ba = dram("d_ba", (TT, P, P))
        d_cw = dram("d_cw", (4, D))

        x = sb("x", [P, TT, D])
        wraw = sb("wraw", [P, 4, TILE])
        whi = sb("whi", [P, 2, TILE], F32R)
        wlo = sb("wlo", [P, 2, TILE], F32R)
        ident = sb("ident", [P, P])
        ones = sb("ones", [P, P])
        NV_NORM, NV_ADAB, NV_C, NV_CONV, NV_DW, NV_CF = 0, 128, 320, 336, 656, 1152
        vec = sb("vec", [P, 1232])
        V_PW1B, V_DWB, V_LNW, V_LNB = NV_CF, NV_CF + 32, NV_CF + 48, NV_CF + 64
        cond = sb("cond", [P, KC])
        mod = sb("mod", [P, 12, KC])
        aff = sb("aff", [P, 4, KC])
        cwc = sb("cwc", [P, 4, KC])
        st = sb("st", [P, 8, TT])
        epsr = sb("epsr", [P, 3])

        ada_st = ExitStack()
        aring = sb("aring", [P, 2, D], at=ada_st)
        aacc = sb("aacc", [P, 2, D], at=ada_st)
        p1 = ExitStack()
        h_hi = sb("h_hi", [P, KC, T], F32R, at=p1)
        h_lo = sb("h_lo", [P, KC, T], F32R, at=p1)
        hf = sb("hf", [P, 2, 4, T], at=p1)
        p1a = ExitStack()
        stage = sb("stage", [P, 12, P], at=p1a)
        y1 = sb("y1", [P, TT, D], at=p1a)
        p1a.close()
        ev = sb("ev", [P, 2, TT, NSL], at=p1)
        cv = sb("cv", [P, 2, 4, T], at=p1)
        sv = sb("sv", [P, 4, T], at=p1)
        sq = sb("sq", [P, 4, T], at=p1)
        rn = sb("rn", [P, 4, T], at=p1)
        kn = sb("kn", [P, 4, T], at=p1)
        kst = sb("kst", [P, 4, T], at=p1)
        zw = sb("zw", [P, TT, NSL], at=p1)
        kks = sb("kks", [P, 4, TT, 32], at=p1)
        ba = sb("ba", [P, TT, P], at=p1)
        gwb = sb("gwb", [P, 4, P], at=p1)
        p1.close()
        ada_st.close()
        p2 = ExitStack()
        oT = sb("oT", [P, HV, T], at=p2)
        p2a = ExitStack()
        ncum = sb("ncum", [P, 2, TT, 4, HQ], at=p2a)
        beta = sb("beta", [P, TT, 4, HQ], at=p2a)
        masks = sb("masks", [P, 2, 2, 3, P], at=p2a)
        m64 = sb("m64", [P, 2, P], at=p2a)
        tri = sb("tri", [P, 4, P], at=p2a)
        epoch = ExitStack()
        ba2 = sb("ba2", [P, TT, P], at=epoch)
        bt = sb("bt", [P, 3, TT, P], at=epoch)
        alog = sb("alog", [P, 2, 64], at=epoch)
        rowsT = sb("rowsT", [P, TT, P], at=epoch)
        rows = sb("rows", [P, T], at=epoch)
        skk = sb("skk", [P, 32, 32], at=epoch)
        srow = sb("srow", [P, 8, 32], at=epoch)
        sdec = sb("sdec", [P, 4, 32, 32], at=epoch)
        stmp = sb("stmp", [P, 2, 2, 32, 32], at=epoch)
        sinv = sb("sinv", [P, 2, 4, 32, 32], at=epoch)
        epoch.close()
        qk = sb("qk", [P, 2, T], at=p2a)
        rr = sb("rr", [P, 8, T], at=p2a)
        vt = sb("vt", [P, TT, 2, P], at=p2a)
        zt = sb("zt", [P, TT, 2, P], at=p2a)
        inv = sb("inv", [P, 2, 4, TT, P], at=p2a)
        mk = sb("mk", [P, 2, 2, 3, P], at=p2a)
        dec = sb("dec", [P, 4, 2, 3, P], at=p2a)
        lm = sb("lm", [P, 4, TT, P], at=p2a)
        wt = sb("wt", [P, 4, TT, P], at=p2a)
        t64 = sb("t64", [P, 4, TT, P], at=p2a)
        rv = sb("rv", [P, 2, 4, P], at=p2a)
        uu = sb("uu", [P, 2, 4, P], at=p2a)
        yh = sb("yh", [P, 4, P], at=p2a)
        osq = sb("osq", [P, 4, P], at=p2a)
        og = sb("og", [P, 4, P], at=p2a)
        oms = sb("oms", [P, 3, 4], at=p2a)
        p2a.close()
        o_hi = sb("o_hi", [P, HV, T], F32R, at=p2)
        o_lo = sb("o_lo", [P, HV, T], F32R, at=p2)
        yg = sb("yg", [P, TT, D], at=p2)
        cwb0 = sb("cwb0", [P, D], at=p2)
        p2.close()
        p3 = ExitStack()
        aring3 = sb("aring3", [P, 2, D], at=p3)
        aacc3 = sb("aacc3", [P, 2, D], at=p3)
        h_hi3 = sb("h_hi3", [P, KC, T], F32R, at=p3)
        h_lo3 = sb("h_lo3", [P, KC, T], F32R, at=p3)
        hf3 = sb("hf3", [P, 2, 4, T], at=p3)
        y = sb("y", [P, TT, D], at=p3)
        cwb = sb("cwb", [P, D], at=p3)
        p3a = ExitStack()
        sg = sb("sg", [P, TT, NSL], at=p3a)
        gg = sb("gg", [P, TT, NSL], at=p3a)
        g_hi = sb("g_hi", [P, 4, T], F32R, at=p3a)
        g_lo = sb("g_lo", [P, 4, T], F32R, at=p3a)
        p3a.close()
        p4 = ExitStack()
        ev4 = sb("ev4", [P, 2, TT, NSL], at=p4)
        lnst = sb("lnst", [P, 2, T], at=p4)
        sg4 = sb("sg4", [P, 4, T], at=p4)
        glu = sb("glu", [P, 4, T], at=p4)
        p4.close()
        p3.close()
        pw2b = ev4[:, :, :, :].rearrange("p a t n -> p (a t n)")
        dwo = y[:, :, :].rearrange("p a (k t) -> p (a k) t", t=T)

        psg = stack.enter_context(nc.psum_tensor("psg", [P, 2, TT, NSL], F32))
        pst = stack.enter_context(nc.psum_tensor("pst", [P, 4, T], F32))
        psn = stack.enter_context(nc.psum_tensor("psn", [P, 4, T], F32))

        ps_kq = psg[:, 0, :, :].rearrange("p a (b t) -> p a b t", t=T)
        ps_w = psg[:, 1, :, :].rearrange("p a (b m) -> p a b m", m=P)
        ps_w = psg[:, 1, :, :].rearrange("p a (b m) -> p (a b) m", m=P)
        ps_t = psn[:, :, :].rearrange("p a (b m) -> p (a b) m", m=P)
        ps_a = pst[:, 0:2, :].rearrange("p a (b m) -> p (a b) m", m=P)
        ps_b = pst[:, 2:4, :].rearrange("p a (b m) -> p (a b) m", m=P)
        ps_o = psg[:, 0, 0, :].rearrange("p (a m) -> p a m", m=P)
        ps_oT = psg[:, 0, 1, :].rearrange("p (a t) -> p a t", t=T)

        w_land = [sem(f"w_land{i}") for i in range(4)]
        w_hi = sem("w_hi")
        w_lo = sem("w_lo")
        w_used = sem("w_used")
        ps_read = sem("ps_read")
        a_land = [sem(f"a_land{i}") for i in range(2)]
        a_zero = sem("a_zero")
        a_used = sem("a_used")
        a_fin = sem("a_fin")
        mod_ok = sem("mod_ok")
        init = sem("init")
        vec_land = sem("vec_land")
        x_land = sem("x_land")
        vec_tr = sem("vec_tr")
        vec_ok = sem("vec_ok")
        cond_ok = sem("cond_ok")
        sq_ok = sem("sq_ok")
        ms_ok = sem("ms_ok")
        rt_ok = sem("rt_ok")
        rs_ok = sem("rs_ok")
        xn_ok = sem("xn_ok")
        pre_tr = sem("pre_tr")
        pre_hf = sem("pre_hf")
        pre_hi = sem("pre_hi")
        pre_lo = sem("pre_lo")
        aff_ok = sem("aff_ok")
        x_up = sem("x_up")
        y_up = sem("y_up")
        tr_done = sem("tr_done")
        conv_done = sem("conv_done")
        tap = sem("tap")
        silu_done = sem("silu_done")
        l2sq_done = sem("l2sq_done")
        nrm_done = sem("nrm_done")
        ln_done = sem("ln_done")
        rn_done = sem("rn_done")
        kn_ready = sem("kn_ready")
        kn_out = sem("kn_out")
        vb_done = sem("vb_done")
        vb_ev = sem("vb_ev")
        zw_done = sem("zw_done")
        z_out = sem("z_out")
        kst_land = sem("kst_land")
        kk_done = sem("kk_done")
        kk_ev = sem("kk_ev")
        kk_out = sem("kk_out")
        ba_ok = sem("ba_ok")
        ba_out = sem("ba_out")
        cwc_ok = sem("cwc_ok")
        cw_out = sem("cw_out")
        cw_land = sem("cw_land")
        gw_land = sem("gw_land")
        c_land = sem("c_land")
        c_init = sem("c_init")
        c_v = sem("c_v")
        c_s = sem("c_s")
        c_p = sem("c_p")
        rows_out = sem("rows_out")
        s_land = sem("s_land")
        inv_out = sem("inv_out")
        qk_land, rr_land, v_land, z_land, inv_land = (sem(n) for n in ("qk_land", "rr_land", "v_land", "z_land", "inv_land"))
        kq_done = sem("kq_done")
        mk_done = sem("mk_done")
        ex_done = sem("ex_done")
        dec_done = sem("dec_done")
        la_done = sem("la_done")
        lm_done = sem("lm_done")
        w_done, wt_done, t_done, t64_done = (sem(n) for n in ("w_done", "wt_done", "t_done", "t64_done"))
        rv_done = sem("rv_done")
        y_done, yc_done, h_done, s_done, u_done, uc_done = (sem(n) for n in ("y_done", "yc_done", "h_done", "s_done", "u_done", "uc_done"))
        x_done, r2_done = sem("x_done"), sem("r2_done")
        o_done, osq_done, oms_done, oln_done, ors_done, on_done, og_done, ot_done, oT_done = (
            sem(n) for n in ("o_done", "osq_done", "oms_done", "oln_done", "ors_done", "on_done", "og_done", "ot_done", "oT_done"))
        osp_hi, osp_lo = sem("osp_hi"), sem("osp_lo")
        g_tr, g_hi_ok, g_lo_ok, y_zero = (sem(n) for n in ("g_tr", "g_hi_ok", "g_lo_ok", "y_zero"))
        t_a, t_g, sg_ok, glu_ok, dw_ok = (sem(n) for n in ("t_a", "t_g", "sg_ok", "glu_ok", "dw_ok"))
        ln_p, ln_v, ln_s = sem("ln_p"), sem("ln_v"), sem("ln_s")
        pb_land = sem("pb_land")
        out_sem = sem("out_sem")

        C_G, C_ROWT, C_ROWS, C_SUB, C_DEC = 5, 13, 14, 17, 21
        C_INV = C_DEC + 4 * 31 + 1
        C_POOL = 22

        block = stack.enter_context(nc.Block())

        def rows4(w, r0, n0):
            return w[ds(r0, KT * P), ds(n0, NSL)].rearrange("(j p) n -> p j n", p=P)

        def tile4(ap):
            return ap.rearrange("p (j n) -> p j n", n=NSL)

        gdn_in, gdn_out = gdn_in_w[0], gdn_out_w[0]
        pw1, pw2 = cf_pw1_w[0], cf_pw2_w[0]

        @block.sync
        def _(sp):
            def load_w(g, slot, src, dst=None):
                if not isinstance(g, int) or g >= 4:
                    sp.wait_ge(w_lo, g - 3)
                sp.dma_start(tile4(wraw[:, slot, :]) if dst is None else dst, src).then_inc(w_land[slot], 16)

            def load_ada(a, ring, flat, k):
                layer, part = flat
                slot = load_ada.slot
                load_ada.slot = 1 - slot
                if not isinstance(a, int) or a >= 2:
                    sp.wait_ge(a_used, a - 1)
                sp.dma_start(ring[:, slot, :], ada_w[layer][ds(k * P, P), ds(part * D, D)]).then_inc(a_land[slot], 16)
            load_ada.slot = 0

            sp.wait_ge(init, 1)
            for r0, src in ((0, norm_w.rearrange("l n (k p) -> (l n k) p", p=P)),
                            (1, ada_b[0:1].rearrange("a (k p) -> (a k) p", p=P)),
                            (2, ada_b[1:2].rearrange("a (k p) -> (a k) p", p=P)),
                            (3, c_in.rearrange("a (k p) -> (a k) p", p=P))):
                sp.dma_start(stage[0:src.shape[0], r0, :], src).then_inc(vec_land, 16)
            sp.dma_start(x[:, :, :], x_in[0].rearrange("(t p) d -> p t d", p=P)).then_inc(x_land, 16)
            conv_rows = gdn_conv_w[0].rearrange("k (b p) -> (k b) p", p=P)
            for n in range(3):
                r = min(P, conv_rows.shape[0] - n * P)
                sp.dma_start(stage[0:r, 4 + n, :], conv_rows[n * P:n * P + r, :]).then_inc(vec_land, 16)
            dw_rows = cf_dw_w[0].rearrange("k (b p) -> (k b) p", p=P)
            for n in range(4):
                r = min(P, dw_rows.shape[0] - n * P)
                sp.dma_start(stage[0:r, 7 + n, :], dw_rows[n * P:n * P + r, :]).then_inc(vec_land, 16)
            r0 = 0
            for src in (cf_pw1_b, cf_dw_b, cf_ln_w, cf_ln_b):
                s = src.rearrange("a (k p) -> (a k) p", p=P)
                sp.dma_start(stage[r0:r0 + s.shape[0], 11, :], s).then_inc(vec_land, 16)
                r0 += s.shape[0]
            for j in range(4):
                sp.dma_start(gwb[:, j, :], gdn_norm_w[0].partition_broadcast(P)).then_inc(gw_land, 16)
            for a in range(2):
                load_ada(a, aring, (0, 0), a)
            load_w(G_BA, 0, gdn_in[:, QKV + VD:QKV + VD + P].rearrange("(j p) n -> p j n", p=P),
                   wraw[:, 0, :].rearrange("p (j n) -> p j n", n=P))
            with sp.Fori(0, 7) as i:
                for s in range(2):
                    load_ada(2 * i + s + 2, aring, (0, 0), 2 * i + s + 2)
            with sp.Fori(0, 8) as i:
                for s in range(2):
                    load_ada(16 + 2 * i + s, aring, (0, 1), 2 * i + s)
            def load_qkv(s):
                for j in range(4):
                    load_w(G_QKV + 4 * s + j, (G_QKV + j) % 4, rows4(gdn_in, j * KT * P, s * NSL))
                    if j == 2:
                        load_ada(32 + s, aring, (0, 2), s)
            load_qkv(0)
            load_qkv(1)
            with sp.Fori(0, NQKV // 2 - 1) as i:
                for s in range(2):
                    load_qkv(2 * i + s + 2)
            for part, z0 in ((3, 0), (4, 4)):
                with sp.Fori(0, 2) as i:
                    for s in range(2):
                        for j in range(4):
                            zs = z0 + 2 * i + s
                            load_w(G_Z + 4 * zs + j, (G_Z + j) % 4, rows4(gdn_in, j * KT * P, QKV + zs * NSL))
                            load_ada(48 + 4 * zs + j, aring, (0, part), 8 * i + 4 * s + j)
            for j in range(4):
                load_w(G_GO + j, (G_GO + j) % 4, rows4(gdn_out, j * KT * P, 0))
            sp.wait_ge(w_used, G_GO)
            sp.wait_ge(ps_read, S_GO)
            sp.wait_ge(z_out, 16 * NZ)
            sp.wait_ge(kk_out, 16 * 4 * 4)
            sp.wait_ge(vb_ev, 8)
            sp.wait_ge(kn_out, 16 * 16)
            sp.wait_ge(mod_ok, 5)
            sp.wait_ge(ba_out, 16)
            sp.dma_start(ba2[:, :, :], d_ba.rearrange("t p n -> p t n")).then_inc(c_land, 16)
            sp.dma_start(alog[:, 0, :], gdn_A_log[0].rearrange("a b -> (a b)").partition_broadcast(P)).then_inc(c_land, 16)
            sp.dma_start(alog[:, 1, :], gdn_dt_bias[0].rearrange("a b -> (a b)").partition_broadcast(P)).then_inc(c_land, 16)
            sp.dma_start(skk[:, :, :].rearrange("p a b -> p (a b)"), d_kk.rearrange("p a b -> p (a b)")).then_inc(c_land, 16)
            sp.wait_ge(c_v, C_ROWS)
            sp.dma_start(d_rows, rows[:, :]).then_inc(rows_out, 16)
            sp.wait_ge(rows_out, 16)
            sp.dma_start(srow[:, :, :], d_rows.rearrange("(c h) (b i) -> (h b) c i", h=HQ, i=32)).then_inc(s_land, 16)
            sp.wait_ge(c_v, C_INV)
            sp.dma_start(d_inv.rearrange("p a c i j -> p (a c i j)"),
                         sinv[:, :, :, :, :].rearrange("p a c i j -> p (a c i j)")).then_inc(inv_out, 16)
            sp.wait_ge(inv_out, 16)
            sp.wait_ge(c_init, C_POOL + 1)
            inv_view = d_inv.rearrange("(h t q) a c i j -> h t q i (a c) j", t=TT, q=4)
            with sp.Fori(0, HQ) as h:
                sp.wait_ge(kq_done, h)
                sp.dma_start(qk[:, 0, :], d_qkn[ds(HQ + h, 1)].rearrange("a p t -> p (a t)")).then_inc(qk_land, 16)
                sp.dma_start(qk[:, 1, :], d_qkn[ds(h, 1)].rearrange("a p t -> p (a t)")).then_inc(qk_land, 16)
                sp.wait_ge(ex_done, h)
                sp.dma_start(rr[:, :, :], d_rows.rearrange("(c h) t -> h c t", h=HQ)[ds(h, 1)].rearrange(
                    "a c t -> (a c) t").partition_broadcast(P)).then_inc(rr_land, 16)
                sp.wait_ge(rv_done, 4 * h)
                sp.dma_start(vt[:, :, :, :].rearrange("p t a m -> p t (a m)"),
                             d_v[:, :, ds(2 * P * h, 2 * P)].rearrange("t p n -> p t n")).then_inc(v_land, 16)
                sp.wait_ge(og_done, h)
                sp.dma_start(zt[:, :, :, :].rearrange("p t a m -> p t (a m)"),
                             d_z[:, :, ds(2 * P * h, 2 * P)].rearrange("t p n -> p t n")).then_inc(z_land, 16)
                sp.wait_ge(t64_done, h)
                for t in range(TT):
                    for q in range(4):
                        sp.dma_start(inv[32 * q:32 * q + 32, :, :, t, 32 * q:32 * q + 32].rearrange("p a c j -> p (a c) j"),
                                     inv_view[ds(h, 1), t, q].rearrange("a i c j -> (a i) c j")).then_inc(inv_land, 16)
            for j in range(4, 8):
                load_w(G_GO + j, (G_GO + j) % 4, rows4(gdn_out, j * KT * P, 0))
            with sp.Fori(1, 4) as n:
                for j in range(8):
                    load_w(G_GO + 8 * n + j, (G_GO + j) % 4, rows4(gdn_out, j * KT * P, n * NSL))

            def load_ffn(layer, g0, with_ada):
                w_in, w_out = ffn_in_w[layer], ffn_out_w[layer]
                for j in range(8):
                    if with_ada and j == 4:
                        sp.wait_ge(x_up, 2)
                        load_ada(80, aring3, (0, 5), 0)
                        load_ada(81, aring3, (0, 5), 1)
                    load_w(g0 + j, (g0 + j) % 4, rows4(w_in, (j % 4) * KT * P, (j // 4) * HID))
                    if with_ada and j >= 4:
                        load_ada(78 + j, aring3, (0, 5), j - 2)
                with sp.Fori(0, (GRP - 1) // 2) as i:
                    at = 0
                    for s in range(2):
                        n = 2 * i + s + 1
                        for j in range(12):
                            if j < 4:
                                src = rows4(w_in, j * KT * P, n * NSL)
                            elif j < 8:
                                src = rows4(w_out, (n - 1) * NSL, (j - 4) * NSL)
                            else:
                                src = rows4(w_in, (j - 8) * KT * P, HID + n * NSL)
                            load_w(g0 + 8 + 24 * i + 12 * s + j, (g0 + j) % 4, src)
                            if with_ada and j >= 3:
                                flat, k = ((1, i), at) if at < 16 else ((0, 5), 6 + 2 * i + at - 16)
                                load_ada(86 + 18 * i + at, aring3, flat, k)
                                at += 1
                for j in range(4):
                    g = g0 + 8 + 12 * (GRP - 1) + j
                    load_w(g, g % 4, rows4(w_out, (GRP - 1) * NSL, j * NSL))

            load_ffn(0, G_F0, True)
            with sp.Fori(0, 4) as i:
                for j in range(8):
                    load_w(G_P1 + 8 * i + j, (G_P1 + j) % 4, rows4(pw1, (j % 4) * KT * P, i * NSL + (j // 4) * D))
                    if j % 2:
                        load_ada(176 + 4 * i + j // 2, aring3, (1, 5), 4 * i + j // 2)
            for j in range(4):
                load_w(G_P2 + j, (G_P2 + j) % 4, rows4(pw2, j * KT * P, 0))
            sp.wait_ge(t_g, 4)
            sp.wait_ge(t_a, 4)
            sp.dma_start(pw2b, cf_pw2_b[0].partition_broadcast(P)).then_inc(pb_land, 16)
            with sp.Fori(1, 4) as n:
                for j in range(4):
                    load_w(G_P2 + 4 * n + j, (G_P2 + j) % 4, rows4(pw2, j * KT * P, n * NSL))
            load_ffn(1, G_F1, False)
            for t in range(TT):
                sp.wait_ge(x_up, 7 + t)
                sp.dma_start(out[0, t * P:(t + 1) * P, :], x[:, t, :]).then_inc(out_sem, 16)
            sp.wait_ge(out_sem, 16 * TT)

        @block.tensor
        def _(pe):
            mm = nc.tensor.matmul

            def tr(dst, src):
                return nc.tensor.transpose(dst, src, ident[:, :])

            def tile(g, slot, ps, a_hi, a_lo, kcs, first, last, width=NSL, ready=None):
                pe.wait_ge(w_lo, g + 1)
                if ready:
                    pe.wait_ge(*ready)
                for j, kc in enumerate(kcs):
                    for t in range(TT):
                        o = ps[:, t, 0:width]
                        ah, al = a_hi[:, kc, t * P:(t + 1) * P], a_lo[:, kc, t * P:(t + 1) * P]
                        wh, wl = (w[:, slot, j * width:(j + 1) * width] for w in (whi, wlo))
                        mm(o, ah, wh, start=first and j == 0, stop=False)
                        mm(o, ah, wl, start=False, stop=False)
                        i = mm(o, al, wh, start=False, stop=last and j == len(kcs) - 1)
                i.then_inc(w_used, 1)

            def pre(n, src):
                for q in range(4):
                    for t in range(TT):
                        if q == 0:
                            pe.wait_ge(xn_ok, TT * n + t + 1)
                    if q >= 2:
                        pe.wait_ge(pre_hf, 4 * n + q - 1)
                    ps = (pst, psn)[q % 2]
                    for j in range(4):
                        for t in range(TT):
                            i = tr(ps[:, j, t * P:(t + 1) * P], src[:, t, (4 * q + j) * P:(4 * q + j + 1) * P])
                    i.then_inc(pre_tr, 1)

            def fin(a_end, acc, n):
                pe.wait_ge(a_used, a_end)
                for kc in range(KC):
                    i = mm(psn[:, 0, kc:kc + 1], acc[:, kc * P:(kc + 1) * P], ones[:, 0:1], start=True, stop=True)
                i.then_inc(a_fin, 1)

            pe.wait_ge(init, 4)
            pe.wait_ge(vec_land, 16 * 15)
            vps = psg[:, :, :, :].rearrange("p a b n -> p (a b n)")
            for n in range(12):
                i = tr(vps[:, n * P:(n + 1) * P], stage[:, n, :])
            i.then_inc(vec_tr, 1)
            fin(16, aacc[:, 0, :], 0)
            pe.wait_ge(mod_ok, 1)
            fin(32, aacc[:, 1, :], 1)
            pe.wait_ge(mod_ok, 2)
            pe.wait_ge(vec_ok, 1)
            pre(0, y1)
            pe.wait_ge(pre_lo, 4)
            pe.wait_ge(sq_ok, 2)
            tile(G_BA, 0, psg[:, 0], h_hi, h_lo, range(KC), True, True, width=P)

            def qkv_slice(s, par, lag1, lag2):
                S = S_QKV + s
                for j in range(4):
                    if j == 0 and (not isinstance(S, int) or S >= 2):
                        pe.wait_ge(ps_read, S - 1)
                    tile(G_QKV + 4 * s + j, (G_QKV + j) % 2, psg[:, (1 + par) % 2], h_hi, h_lo,
                         range(4 * j, 4 * j + 4), j == 0, j == 3)
                    lags(s, par, j, lag1, lag2)

            def lags(s, par, j, lag1, lag2):
                if j == 0 and lag1:
                    pe.wait_ge(ps_read, S_QKV + s)
                    if not isinstance(s, int) or s >= 2:
                        pe.wait_ge(conv_done, s - 1)
                    for b in range(4):
                        for t in range(TT):
                            i = tr(pst[:, b, t * P:(t + 1) * P], ev[:, 1 - par, t, b * P:(b + 1) * P])
                    i.then_inc(tr_done, 1)
                if j == 1 and lag2 == "n":
                    pe.wait_ge(l2sq_done, s - 1)
                    if not isinstance(s, int) or s >= 3:
                        pe.wait_ge(ln_done, s - 2)
                    for b in range(2):
                        i = mm(psn[:, 2 * b:2 * b + 2, :], ones[:, :], sq[:, 2 * b:2 * b + 2, :], start=True, stop=True)
                    i.then_inc(nrm_done, 1)
                if j == 1 and lag2 == "v":
                    pe.wait_ge(silu_done, s - 1)
                    pe.wait_ge(ln_done, 8)
                    if not isinstance(s, int) or s > 10:
                        pe.wait_ge(vb_ev, s - 10)
                    vps = psn[:, :, :].rearrange("p (t a) b -> p t (a b)", t=TT)
                    for b in range(4):
                        for t in range(TT):
                            i = tr(vps[:, t, b * P:(b + 1) * P], sv[:, b, t * P:(t + 1) * P])
                    i.then_inc(vb_done, 1)

            qkv_slice(0, 0, False, None)
            qkv_slice(1, 1, True, None)
            with pe.Fori(0, 4) as i:
                for s in range(2):
                    qkv_slice(2 + 2 * i + s, s, True, "n")
            with pe.Fori(0, 3) as i:
                for s in range(2):
                    qkv_slice(10 + 2 * i + s, s, True, "v")

            def z_slice(z, par, lag1=False, lag2=None, kk=False):
                S = S_Z + z
                pe.wait_ge(ps_read, S - 1)
                for j in range(4):
                    tile(G_Z + 4 * z + j, (G_Z + j) % 2, psg[:, (1 + par) % 2], h_hi, h_lo,
                         range(4 * j, 4 * j + 4), j == 0, j == 3)
                    lags(NQKV + z, par, j, lag1, lag2)
                    if j == 1 and kk:
                        pe.wait_ge(kst_land, 16 * (z - 3))
                        pe.wait_ge(conv_done, NQKV)
                        pe.wait_ge(kk_ev, 4 * (z - 4))
                        for b in range(4):
                            for t in range(TT):
                                k = kst[:, b, t * P:(t + 1) * P]
                                i = mm(pst[:, b, t * P:(t + 1) * P], k, k, start=True, stop=True)
                        i.then_inc(kk_done, 1)

            z_slice(0, 0, True, "v")
            z_slice(1, 1, False, "v")
            pe.wait_ge(vb_ev, 8)
            fin(48, aacc[:, 0, :], 2)
            z_slice(2, 0)
            z_slice(3, 1)
            with pe.Fori(2, 4) as i:
                for s in range(2):
                    z_slice(2 * i + s, s, kk=True)
            pe.wait_ge(mod_ok, 3)
            fin(64, aacc[:, 1, :], 3)
            pe.wait_ge(mod_ok, 4)
            fin(80, aacc[:, 0, :], 4)

            pe.wait_ge(mod_ok, 5)
            pe.wait_ge(ps_read, S_GO)
            pe.wait_ge(kk_ev, 16)
            pe.wait_ge(c_init, C_POOL)
            pe.wait_ge(c_v, C_G)
            incl = psg[:, 0, 0, 0:P].rearrange("p (t c) -> p t c", t=TT)
            cross = psg[:, 0, 0, P:2 * P].rearrange("p (t c) -> p t c", t=TT)
            for d in range(2):
                g = bt[:, 2, :, 64 + 32 * d:96 + 32 * d]
                mm(incl[:, :, 32 * d:32 * d + 32], tri[:, 2 * d, :], g, start=True, stop=True)
                i = mm(cross[:, :, 32 * d:32 * d + 32], tri[:, 2 * d + 1, :], g, start=True, stop=True)
            i.then_inc(c_p, 1)
            pe.wait_ge(c_v, C_ROWT)
            for t in range(TT):
                i = tr(psg[:, 0, 1, t * P:(t + 1) * P], rowsT[:, t, :])
            i.then_inc(c_p, 1)
            pe.wait_ge(c_v, C_ROWS)

            with pe.Fori(0, HQ) as h:
                pe.wait_ge(qk_land, 32 * (h + 1))
                pe.wait_ge(oT_done, h)
                for kind in range(2):
                    for jt in range(TT):
                        i = mm(ps_kq[:, kind, jt, :], qk[:, 0, jt * P:(jt + 1) * P], qk[:, kind, :], start=True, stop=True)
                i.then_inc(kq_done, 1)
                pe.wait_ge(lm_done, 2 * (h + 1))
                pe.wait_ge(inv_land, 128 * (h + 1))
                for c in range(4):
                    for t in range(TT):
                        i = mm(ps_w[:, 2 * c + t, :], lm[:, c, t, :], inv[:, 0, c, t, :], start=True, stop=True)
                i.then_inc(w_done, 1)
                pe.wait_ge(wt_done, h + 1)
                for c in range(4):
                    for t in range(TT):
                        i = mm(ps_t[:, 2 * c + t, :], wt[:, c, t, :], inv[:, 1, c, t, :], start=True, stop=True)
                i.then_inc(t_done, 1)
                pe.wait_ge(rv_done, 4 * (h + 1))
                for o in range(2):
                    if o == 0:
                        pe.wait_ge(t64_done, h + 1)
                    else:
                        pe.wait_ge(r2_done, 2 * (h + 1))
                    for c in range(4):
                        t = o if c < 2 else 1 - o
                        i = mm(ps_a[:, c, :], t64[:, c, t, :], rv[:, o, c, :], start=True, stop=True)
                    i.then_inc(y_done, 1)
                    pe.wait_ge(yc_done, 4 * h + 2 * o + 2)
                    for c in range(4):
                        t = o if c < 2 else 1 - o
                        i = mm(ps_b[:, c, :], dec[:, c, 0, 2 * t, :], yh[:, c, :], start=True, stop=True)
                    i.then_inc(h_done, 1)
                    pe.wait_ge(s_done, 4 * h + 2 * o + 2)
                    for c in range(4):
                        t = o if c < 2 else 1 - o
                        i = mm(ps_a[:, c, :], t64[:, c, t, :], rv[:, o, c, :], start=True, stop=True)
                    i.then_inc(u_done, 1)
                    pe.wait_ge(uc_done, 2 * h + o + 1)
                    if o == 0:
                        for c in range(4):
                            i = mm(ps_b[:, c, :], dec[:, c, 0, 1, :], uu[:, 0, c, :], start=True, stop=True)
                        i.then_inc(x_done, 1)
                for t in range(TT):
                    for v in range(2):
                        terms = []
                        for d in range(2):
                            for o in range(2):
                                tj = o if d == 0 else 1 - o
                                if tj == t:
                                    terms.append((2 * t, 2 * d + v, o))
                                elif o == 0:
                                    terms.append((1, 2 * d + v, o))
                        for n, (seg, c, o) in enumerate(terms):
                            i = mm(ps_o[:, 2 * t + v, :], dec[:, c, 1, seg, :], uu[:, o, c, :],
                                   start=n == 0, stop=n == len(terms) - 1)
                i.then_inc(o_done, 1)
                pe.wait_ge(og_done, h + 1)
                for v in range(2):
                    for t in range(TT):
                        i = tr(ps_oT[:, v, t * P:(t + 1) * P], og[:, 2 * t + v, :])
                i.then_inc(ot_done, 1)
            pe.wait_ge(oT_done, HQ)

            with pe.Fori(0, 2) as i:
                for s in range(2):
                    n = 2 * i + s
                    pe.wait_ge(ps_read, S_GO + n - 1)
                    for j in range(8):
                        tile(G_GO + 8 * n + j, (G_GO + j) % 2, psg[:, (S_GO + s) % 2], o_hi, o_lo,
                             range(4 * j, 4 * j + 4), j == 0, j == 7, ready=(osp_lo, j + 1))

            def ffn(f, g0, s0, n_pre):
                def sl(S, par, g, kcs_tiles, a_hi, a_lo, ready=None, after=None):
                    pe.wait_ge(ps_read, S - 1)
                    for j, kcs in enumerate(kcs_tiles):
                        tile(g + j, (g0 + par[1] + j) % 2, psg[:, (s0 + par[0]) % 2], a_hi, a_lo, kcs, j == 0,
                             j == len(kcs_tiles) - 1, ready=ready and ready(j))
                        if after:
                            after(j)
                whole = [range(4 * j, 4 * j + 4) for j in range(4)]
                sl(s0, (0, 0), g0, whole, h_hi3, h_lo3, ready=lambda j: (pre_lo, 4 * n_pre + j + 1))
                sl(s0 + 1, (1, 4), g0 + 4, whole, h_hi3, h_lo3)

                def turn(n):
                    pe.wait_ge(ps_read, s0 + 6 * n + 2)
                    pe.wait_ge(g_lo_ok, GRP * f + n)
                    for b in range(4):
                        for t in range(TT):
                            i = tr(pst[:, b, t * P:(t + 1) * P], gg[:, t, b * P:(b + 1) * P])
                    i.then_inc(g_tr, 1)

                def outs(n, S, par, g, gpar):
                    for j in range(4):
                        sl(S + j, (par + j, gpar + j), g + j, [range(4)], g_hi, g_lo,
                           ready=lambda _: (g_lo_ok, GRP * f + n + 1))

                with pe.Fori(0, (GRP - 1) // 2) as i:
                    for s in range(2):
                        n = 2 * i + s + 1
                        S, g = s0 + 2 + 12 * i + 6 * s, g0 + 8 + 24 * i + 12 * s
                        sl(S, (0, 0), g, whole, h_hi3, h_lo3, after=lambda j: turn(n - 1) if j == 0 else None)
                        outs(n - 1, S + 1, 1, g + 4, 0)

                        def last(j):
                            if f == 0 and s == 1 and j == 2:
                                pe.wait_ge(mod_ok, 5 + i)
                                fin(102 + 18 * i, aacc3[:, 1, :], None)
                        sl(S + 5, (1, 0), g + 8, whole, h_hi3, h_lo3, after=last)
                turn(GRP - 1)
                if f == 0:
                    pe.wait_ge(mod_ok, 10)
                    fin(176, aacc3[:, 0, :], None)
                outs(GRP - 1, s0 + 2 + 6 * (GRP - 1), 0, g0 + 8 + 12 * (GRP - 1), 0)

            pre(1, y)
            ffn(0, G_F0, S_F0, 1)
            pre(2, y)
            def turn2(ready, src, dst, done, free):
                pe.wait_ge(*ready)
                if free:
                    pe.wait_ge(*free)
                for b in range(4):
                    for t in range(TT):
                        i = tr(dst[:, b, t * P:(t + 1) * P], src[:, t, b * P:(b + 1) * P])
                i.then_inc(done, 1)

            def pw1_pair(n, lag):
                for j in range(8):
                    if j % 4 == 0:
                        pe.wait_ge(ps_read, S_P1 + 2 * n + j // 4 - 1)
                    tile(G_P1 + 8 * n + j, (G_P1 + j) % 2, psg[:, (S_P1 + j // 4) % 2], h_hi3, h_lo3,
                         range(4 * (j % 4), 4 * (j % 4) + 4), j % 4 == 0, j % 4 == 3,
                         ready=(pre_lo, 8 + j % 4 + 1))
                    if j == 0 and lag:
                        turn2((ps_read, S_P1 + 2 * n), ev4[:, 1], psn, t_g, (sg_ok, n - 1))
                    if j == 4:
                        turn2((ps_read, S_P1 + 2 * n + 1), ev4[:, 0], pst, t_a, (glu_ok, n))
            pw1_pair(0, False)
            with pe.Fori(1, 4) as i:
                pw1_pair(i, True)
            turn2((ps_read, S_P2), ev4[:, 1], psn, t_g, (sg_ok, 3))
            pe.wait_ge(sg_ok, 4)
            fin(192, aacc3[:, 0, :], None)
            pe.wait_ge(dw_ok, 4)
            pe.wait_ge(glu_ok, 4)
            for kc in range(KC):
                i = mm(pst[:, 0, :], ones[:, :], dwo[:, kc, :], start=kc == 0, stop=kc == KC - 1)
            i.then_inc(ln_p, 1)
            for q in range(4):
                pe.wait_ge(ln_s, q + 1)
                for j in range(4):
                    i = mm(pst[:, 2, :], ones[:, :], hf3[:, q % 2, j, :], start=q + j == 0, stop=q + j == 6)
                i.then_inc(ln_p, 1)
            with pe.Fori(0, 2) as i:
                for s in range(2):
                    n = 2 * i + s
                    pe.wait_ge(ps_read, S_P2 + n - 1)
                    for j in range(4):
                        tile(G_P2 + 4 * n + j, (G_P2 + j) % 2, psg[:, (S_P2 + s) % 2], h_hi3, h_lo3,
                             range(4 * j, 4 * j + 4), j == 0, j == 3, ready=(pre_lo, 12 + j + 1))
            pre(3, y)
            ffn(1, G_F1, S_F1, 4)

        @block.vector
        def _(dve):
            tt, ts, stt = nc.vector.tensor_tensor, nc.vector.tensor_scalar, nc.vector.scalar_tensor_tensor

            def lo(g, j):
                dve.wait_ge(w_hi, g + 1)
                tt(wlo[:, j % 2, :], wraw[:, j % 4, :], whi[:, j % 2, :].bitcast(F32), SUB).then_inc(w_lo, 1)

            def ada(a, par, ring, acc, k, first=False):
                dve.wait_ge(a_land[par], 8 * (a - par) + 16)
                c = cond[:, ds(k, 1)]
                if first:
                    ts(acc, ring[:, par, :], c, None, MUL).then_inc(a_used, 1)
                else:
                    dve.wait_ge(a_used, a)
                    stt(acc, ring[:, par, :], c, acc, MUL, ADD).then_inc(a_used, 1)

            def mod_add(n, flat):
                dve.wait_ge(a_fin, n)
                tt(mod[:, ds(flat, 1), :].rearrange("p a k -> p (a k)"), psn[:, 0, 0:KC],
                   vec[:, ds(NV_ADAB + flat * KC, KC)], ADD).then_inc(mod_ok, 1)

            def norm_stat(k, then):
                for t in range(TT):
                    dve.wait_ge(sq_ok, TT * k + t + 1)
                    ts(st[:, k, t:t + 1], st[:, k, t:t + 1], 1.0 / D, RMS_EPS, MUL, ADD).then_inc(ms_ok, 1)
                for t in range(TT):
                    dve.wait_ge(rt_ok, TT * k + t + 1)
                    nc.vector.reciprocal(st[:, k, t:t + 1], st[:, k, t:t + 1]).then_inc(rs_ok, 1)
                    dve.wait_ge(rs_ok, TT * k + t + 1)
                    then(t)

            def pre(n, xn, hi, lo_, hfb, mods):
                def normalise(t):
                    ts(xn[:, t, :], x[:, t, :], st[:, 2 * n, t:t + 1], None, MUL).then_inc(xn_ok, 1)
                norm_stat(2 * n, normalise)
                dve.wait_ge(mod_ok, mods)
                stt(aff[:, n, :], mod[:, 3 * n + 1, :], 1.0, vec[:, NV_NORM + 2 * n * KC:NV_NORM + (2 * n + 1) * KC],
                    ADD, MUL).then_inc(aff_ok, 1)
                dve.wait_ge(aff_ok, n + 1)
                for q in range(4):
                    dve.wait_ge(pre_tr, 4 * n + q + 1)
                    if q >= 2:
                        dve.wait_ge(pre_hi, 4 * n + q - 1)
                    for j in range(4):
                        kc = 4 * q + j
                        i = ts(hfb[:, q % 2, j, :], (pst, psn)[q % 2][:, j, :], aff[:, n, kc:kc + 1],
                               mod[:, 3 * n, kc:kc + 1], MUL, ADD)
                    i.then_inc(pre_hf, 1)
                    dve.wait_ge(pre_hf, 4 * n + q + 1)
                    dve.wait_ge(pre_hi, 4 * n + q + 1)
                    tt(lo_[:, 4 * q:4 * q + 4, :], hfb[:, q % 2], hi[:, 4 * q:4 * q + 4, :].bitcast(F32),
                       SUB).then_inc(pre_lo, 1)

            def post(n, yb, cw):
                dve.wait_ge(cw_land, 16 * (n + 1))

                def update(t):
                    stt(yb[:, t, :], yb[:, t, :], st[:, 2 * n + 1, t:t + 1], cw[:, :], MUL, MUL).then_inc(y_up, 1)
                    dve.wait_ge(y_up, TT * n + t + 1)
                    tt(x[:, t, :], x[:, t, :], yb[:, t, :], ADD).then_inc(x_up, 1)
                norm_stat(2 * n + 1, update)

            def cw_col(n, mods):
                dve.wait_ge(mod_ok, mods)
                stt(cwc[:, n, :], mod[:, 3 * n + 2, :], 1.0,
                    vec[:, NV_NORM + (2 * n + 1) * KC:NV_NORM + (2 * n + 2) * KC], ADD, MUL).then_inc(cwc_ok, 1)

            dve.wait_ge(vec_tr, 1)
            vps = psg[:, :, :, :].rearrange("p a b n -> p (a b n)")
            for n, (at, w) in enumerate(((0, 128), (128, 96), (224, 96), (320, 16), (336, 128), (464, 128), (592, 64),
                                         (656, 128), (784, 128), (912, 128), (1040, 112), (1152, 80))):
                i = nc.vector.tensor_copy(vec[:, at:at + w], vps[:, n * P:n * P + w])
            i.then_inc(vec_ok, 1)
            for n in range(2):
                nc.vector.memset(aacc[:, n, :], 0.0).then_inc(a_zero, 1)
            dve.wait_ge(cond_ok, 1)
            dve.wait_ge(a_zero, 2)
            for n in range(2):
                with dve.Fori(0, 8) as i:
                    for s in range(2):
                        ada(16 * n + 2 * i + s, s, aring, aacc[:, n, :], 2 * i + s)
                mod_add(n + 1, n)
            pre(0, y1, h_hi, h_lo, hf, 2)
            nc.vector.memset(aacc[:, 0, :], 0.0).then_inc(a_zero, 1)
            lo(0, 0)
            lo(1, 1)
            dve.wait_ge(w_used, 1)
            nc.vector.tensor_copy(ba[:, :, :], psg[:, 0, :, 0:P]).then_inc(ps_read, 1)
            dve.wait_ge(a_zero, 3)

            taps = Tally(tap)

            def conv(s, par, half):
                if half == 0:
                    dve.wait_ge(tr_done, s + 1)
                    if not isinstance(s, int) or s >= 2:
                        dve.wait_ge(silu_done, s - 1)
                for n, k in enumerate((2, 0, 1, 3, 4)):
                    off = k - 2
                    a, b = max(0, -off), T - max(0, off)
                    if n:
                        dve.wait_ge(tap, taps.at())
                    for blk in (2 * half, 2 * half + 1):
                        w = vec[:, ds(NV_CONV + k * (QKV // P) + 4 * s + blk, 1)]
                        src, dst = pst[:, blk, a + off:b + off], cv[:, par, blk, a:b]
                        if n == 0:
                            i = ts(dst, src, w, None, MUL)
                        else:
                            i = stt(dst, src, w, dst, MUL, ADD)
                        if half and n == 4 and blk == 3:
                            i.then_inc(conv_done, 1)
                        else:
                            taps.inc(i)

            def qkv_slice(s, par, lag):
                g = G_QKV + 4 * s
                if not (isinstance(s, int) and s == 0):
                    lo(g, G_QKV)
                lo(g + 1, G_QKV + 1)
                lo(g + 2, G_QKV + 2)
                if lag:
                    conv(s - 1, 1 - par, 0)
                lo(g + 3, G_QKV + 3)
                if lag:
                    conv(s - 1, 1 - par, 1)
                ada(32 + s, par, aring, aacc[:, 0, :], s)

            qkv_slice(0, 0, False)
            qkv_slice(1, 1, True)
            with taps.loop(dve, 0, 7, 2 * 19) as i:
                for s in range(2):
                    qkv_slice(2 + 2 * i + s, s, True)

            def z_slice(z, par, n, lag=False, extra=None):
                for j in range(4):
                    lo(G_Z + 4 * z + j, G_Z + j)
                    if lag and j >= 2:
                        conv(NQKV - 1, 1, j - 2)
                    if extra and j == 0:
                        extra()
                    ada(48 + 4 * z + j, j % 2, aring, aacc[:, n, :], (4 * z + j) if isinstance(z, int) else z * 4 + j - 16)

            nc.vector.memset(aacc[:, 1, :], 0.0).then_inc(a_zero, 1)
            dve.wait_ge(a_zero, 4)
            z_slice(0, 0, 1, lag=True)
            z_slice(1, 1, 1)
            z_slice(2, 0, 1, extra=lambda: mod_add(3, 2))
            z_slice(3, 1, 1)
            nc.vector.memset(aacc[:, 0, :], 0.0).then_inc(a_zero, 1)
            dve.wait_ge(a_zero, 5)
            with dve.Fori(2, 4) as i:
                for s in range(2):
                    z_slice(2 * i + s, s, 0)
            mod_add(4, 3)
            mod_add(5, 4)
            cw_col(0, 5)

            pr = Tally(c_v)
            split = "p (d h v) -> p d v h"

            def dvh(ap):
                return ap.rearrange(split, d=2, v=2)

            def dv(ap):
                return ap.rearrange("p (d v) h -> p d v h", d=2)
            dve.wait_ge(c_land, 64)
            pr.inc(nc.vector.tensor_copy(bt[:, 0, :, 0:64], ba2[:, :, 0:64]))
            pr.inc(tt(bt[:, 0, :, 64:128], ba2[:, :, 64:128], alog[:, 1:2, :].broadcast_to([P, TT, 64]), ADD))
            pr.wait(dve)
            pr.inc(ts(bt[:, 0, :, 64:128], bt[:, 0, :, 64:128], -1.0, None, MUL))
            dve.wait_ge(c_s, 4)
            pr.wait(dve)
            flat = "p a b -> p (a b)"
            pr.inc(stt(bt[:, 2].rearrange(flat), bt[:, 0].rearrange(flat), 0.0, bt[:, 1].rearrange(flat), MIN, SUB))
            pr.wait(dve)
            pr.inc(tt(bt[:, 2, :, 64:128], bt[:, 2, :, 64:128], alog[:, 0:1, :].broadcast_to([P, TT, 64]), MUL))
            assert pr.n == C_G
            incl = psg[:, 0, 0, 0:P].rearrange("p (t c) -> p t c", t=TT)
            cross = psg[:, 0, 0, P:2 * P].rearrange("p (t c) -> p t c", t=TT)
            dve.wait_ge(c_p, 1)
            dve.wait_ge(c_init, C_POOL)
            for t in range(TT):
                pr.inc(ts(dv(ncum[:, 0, t]), dvh(incl[:, t]), -1.0, None, MUL))
                pr.inc(nc.vector.tensor_copy(dv(ncum[:, 1, t]), dvh(cross[:, t])))
            for t in range(TT):
                r = rowsT[:, t, :].rearrange("p (d v k h) -> p d v k h", d=2, v=2, k=2)
                pr.inc(tt(r[:, :, :, 0, :], dvh(incl[:, t]), dvh(bt[:, 2, t, 0:64]), ADD))
                pr.inc(nc.vector.tensor_copy(r[:, :, :, 1, :], dvh(incl[:, t])))
            assert pr.n == C_ROWT
            dve.wait_ge(c_p, 2)
            pr.inc(nc.vector.tensor_copy(rows[:, :], psg[:, 0, 1, 0:T]))
            assert pr.n == C_ROWS
            dve.wait_ge(s_land, 16)
            sr4 = srow[:, :, :].rearrange("p (c k) i -> p c k i", k=2)
            for d in range(2):
                pr.inc(tt(sdec[:, 2 * d:2 * d + 2],
                          sr4[:, 2 * d:2 * d + 2, 0, :].unsqueeze(3).broadcast_to([P, 2, 32, 32]),
                          sr4[:, 2 * d:2 * d + 2, 1, :].unsqueeze(2).broadcast_to([P, 2, 32, 32]), SUB))
            pr.wait(dve)
            sflat = sdec[:, :, :, :].rearrange("p c i j -> p (c i j)")
            pr.inc(ts(sflat, sflat, 0.0, None, MIN))
            assert pr.n == C_SUB
            dve.wait_ge(c_s, 7)
            for c in range(4):
                s1 = sdec[:, c].rearrange("p i j -> p (i j)")
                pr.inc(stt(s1, skk[:, :, :].rearrange("p i j -> p (i j)"), -1.0, s1, MUL, MUL))
            assert pr.n == C_DEC
            for n in range(1, 32):
                pr.wait(dve)
                for d in range(2):
                    r, a = (n, 0) if d == 0 else (31 - n, 32 - n)
                    pr.inc(tt(stmp[:, d, :, 0:n, 0:n],
                              sdec[:, 2 * d:2 * d + 2, r, a:a + n].unsqueeze(2).broadcast_to([P, 2, n, n]),
                              sinv[:, 0, 2 * d:2 * d + 2, a:a + n, a:a + n].rearrange("p v j c -> p v c j"), MUL))
                pr.wait(dve)
                for d in range(2):
                    r, a = (n, 0) if d == 0 else (31 - n, 32 - n)
                    pr.inc(nc.vector.tensor_reduce(sinv[:, 0, 2 * d:2 * d + 2, r, a:a + n], stmp[:, d, :, 0:n, 0:n],
                                                   axis=AX, op=ADD))
            pr.wait(dve)
            pr.inc(nc.vector.tensor_copy(sinv[:, 1].rearrange("p c i j -> p c j i"), sinv[:, 0]))
            assert pr.n == C_INV

            mkf = mk[:, :, :, :, :].rearrange("p d k s m -> p d k (s m)")
            mmf = masks[:, :, :, :, :].rearrange("p d k s m -> p d k (s m)")
            kqf = psg[:, 0, :, :]
            with dve.Fori(0, HQ) as h:
                dve.wait_ge(rr_land, 16 * (h + 1))
                dve.wait_ge(o_done, h)
                for c in range(4):
                    for seg, t, kind, tj in ((0, 0, 0, 0), (2, 1, 0, 1), (1, 1 - c // 2, 1, c // 2)):
                        i = ts(dec[:, c, :, seg, :], rr[:, 2 * c:2 * c + 2, t * P:(t + 1) * P],
                               ncum[:, kind, tj, c, ds(h, 1)], 0.0, ADD, MIN)
                i.then_inc(ex_done, 1)
                dve.wait_ge(kq_done, h + 1)
                for d, dst, src in ((0, 0, 0), (1, 1, 2)):
                    w0 = d * P
                    tt(mkf[:, d, :, w0:w0 + 2 * P], kqf[:, :, src * P:(src + 2) * P], mmf[:, d, :, w0:w0 + 2 * P], MUL)
                    n0, nsrc = ((2, 3) if d == 0 else (0, 0))
                    i = tt(mkf[:, d, :, n0 * P:(n0 + 1) * P], kqf[:, :, nsrc * P:(nsrc + 1) * P],
                           mmf[:, d, :, n0 * P:(n0 + 1) * P], MUL)
                i.then_inc(mk_done, 1)
                dve.wait_ge(mk_done, h + 1)
                dve.wait_ge(dec_done, h + 1)
                for c in range(4):
                    f = dec[:, c].rearrange("p k s m -> p (k s m)")
                    i = tt(f, f, mk[:, c // 2].rearrange("p k s m -> p (k s m)"), MUL)
                i.then_inc(la_done, 1)
                dve.wait_ge(la_done, h + 1)
                dve.wait_ge(w_done, h)
                for d in range(2):
                    for v in range(2):
                        i = tt(lm[:, 2 * d + v, :, :], dec[:, 2 * d + v, 0, 0:3:2, :],
                               m64[:, d:d + 1, :].broadcast_to([P, TT, P]), MUL)
                    i.then_inc(lm_done, 1)
                dve.wait_ge(t_done, h + 1)
                tt(t64[:, :, :, :].rearrange("p c t m -> p (c t) m"), ps_t,
                   inv[:, 1].rearrange("p c t m -> p (c t) m"), ADD).then_inc(t64_done, 1)
                for o in range(2):
                    dve.wait_ge(h_done, 2 * h + o + 1)
                    if o == 0:
                        dve.wait_ge(rv_done, 4 * (h + 1))
                    for d in range(2):
                        q = slice(64, P) if d == 0 else slice(0, 64)
                        tt(rv[q, o, 2 * d:2 * d + 2, :], ps_b[q, 2 * d:2 * d + 2, :], rv[q, o, 2 * d:2 * d + 2, :],
                           ADD).then_inc(s_done, 1)
                    if o == 0:
                        dve.wait_ge(x_done, h + 1)
                        for d in range(2):
                            tt(rv[:, 1, 2 * d:2 * d + 2, :], ps_b[:, 2 * d:2 * d + 2, :], rv[:, 1, 2 * d:2 * d + 2, :],
                               ADD).then_inc(r2_done, 1)
                dve.wait_ge(osq_done, h + 1)
                nc.vector.tensor_reduce(oms[:, 0, :], osq[:, :, :], axis=AX, op=ADD).then_inc(oms_done, 1)
                dve.wait_ge(ors_done, h + 1)
                dve.wait_ge(z_land, 16 * (h + 1))
                dve.wait_ge(ot_done, h)
                tt(og[:, :, :], ps_o, oms[:, 2, :].unsqueeze(2).broadcast_to([P, 4, P]), MUL).then_inc(on_done, 1)
                dve.wait_ge(on_done, h + 1)
                tt(og[:, :, :], og[:, :, :], zt[:, :, :, :].rearrange("p t a m -> p (t a) m"), MUL).then_inc(og_done, 1)

            dve.wait_ge(oT_done, HQ)
            lo(G_GO, G_GO)
            lo(G_GO + 1, G_GO + 1)
            for q in range(8):
                dve.wait_ge(osp_hi, q + 1)
                tt(o_lo[:, 4 * q:4 * q + 4, :], oT[:, 4 * q:4 * q + 4, :], o_hi[:, 4 * q:4 * q + 4, :].bitcast(F32),
                   SUB).then_inc(osp_lo, 1)
            for j in range(2, 8):
                lo(G_GO + j, G_GO + j)
            with dve.Fori(1, 4) as n:
                for j in range(8):
                    lo(G_GO + 8 * n + j, G_GO + j)
            post(0, yg, cwb0)
            pre(1, y, h_hi3, h_lo3, hf3, 5)

            def ffn(f, g0, s0):
                nm = GRP * f
                nc.vector.memset(y[:, :, :], 0.0).then_inc(y_zero, 1)
                dve.wait_ge(y_zero, f + 1)

                def mul(n, S, g_end):
                    dve.wait_ge(w_used, g_end)
                    dve.wait_ge(ps_read, S)
                    if f or not isinstance(n, int):
                        dve.wait_ge(g_tr, nm + n)
                    tt(gg[:, :, :], psg[:, (s0 + 1) % 2], sg[:, :, :], MUL).then_inc(ps_read, 1)

                def g_low(n):
                    dve.wait_ge(g_hi_ok, nm + n + 1)
                    tt(g_lo[:, :, :], pst[:, :, :], g_hi[:, :, :].bitcast(F32), SUB).then_inc(g_lo_ok, 1)

                def y_sum(S, g_end, par, j, n):
                    dve.wait_ge(w_used, g_end)
                    yj = y[:, :, j * NSL:(j + 1) * NSL]
                    dve.wait_ge(ps_read, S)
                    tt(yj, psg[:, (s0 + par) % 2], yj, ADD).then_inc(ps_read, 1)

                for j in range(8):
                    lo(g0 + j, g0 + j)
                    if f == 0 and j < 6:
                        ada(80 + j, j % 2, aring3, aacc3[:, 0, :], j, first=j == 0)
                with dve.Fori(0, (GRP - 1) // 2) as i:
                    at = 0
                    for s in range(2):
                        n = 2 * i + s + 1
                        S, g = s0 + 2 + 12 * i + 6 * s, g0 + 8 + 24 * i + 12 * s
                        for j in range(12):
                            if 6 <= j < 10:
                                y_sum(S + j - 5, g + j - 1, j - 5, j - 6, n - 1)
                            lo(g + j, g0 + j)
                            if j == 0:
                                mul(n - 1, S - 1, g)
                            if j == 2:
                                g_low(n - 1)
                            if f == 0 and j >= 3:
                                if at < 16:
                                    ada(86 + 18 * i + at, at % 2, aring3, aacc3[:, 1, :], at, first=at == 0)
                                else:
                                    ada(86 + 18 * i + at, at % 2, aring3, aacc3[:, 0, :], 6 + 2 * i + at - 16)
                                at += 1
                    if f == 0:
                        mod_add(6 + i, 6 + i)
                gl, Sl = g0 + 8 + 12 * (GRP - 1), s0 + 2 + 6 * (GRP - 1)
                lo(gl, g0)
                mul(GRP - 1, Sl - 1, gl)
                lo(gl + 1, g0 + 1)
                g_low(GRP - 1)
                if f == 0:
                    mod_add(11, 5)
                    cw_col(1, 11)
                for j in range(4):
                    y_sum(Sl + j, gl + j + 1, j, j, GRP - 1)
                    if j < 2:
                        lo(gl + j + 2, g0 + j + 2)

            ffn(0, G_F0, S_F0)
            post(1, y, cwb)
            pre(2, y, h_hi3, h_lo3, hf3, 11)
            cw_col(2, 11)
            nc.vector.memset(aacc3[:, 0, :], 0.0).then_inc(a_zero, 1)
            dve.wait_ge(a_zero, 6)
            dwt = Tally(tap, taps.n)

            def unit(n):
                dve.wait_ge(sg_ok, n + 1)
                dve.wait_ge(t_a, n + 1)
                dve.wait_ge(dw_ok, n)
                for b in range(4):
                    i = stt(glu[:, b, :], pst[:, b, :], vec[:, ds(V_PW1B + 4 * n + b, 1)], sg4[:, b, :], ADD, MUL)
                i.then_inc(glu_ok, 1)
                dve.wait_ge(glu_ok, n + 1)

            order = [(n, k) for n, k in enumerate([CTAPS // 2] + [k for k in range(CTAPS) if k != CTAPS // 2])]

            def dw(n, part):
                for m, k in part:
                    off = k - CTAPS // 2
                    a, e = max(0, -off), T - max(0, off)
                    if m:
                        dve.wait_ge(tap, dwt.at())
                    for b in range(4):
                        w = vec[:, ds(NV_DW + k * KC + 4 * n + b, 1)]
                        src = glu[:, b, a + off:e + off]
                        dst = dwo[:, ds(4 * n + b, 1), a:e].rearrange("p a t -> p (a t)")
                        if m == 0:
                            i = ts(dst, src, w, vec[:, ds(V_DWB + 4 * n + b, 1)], MUL, ADD)
                        else:
                            i = stt(dst, src, w, dst, MUL, ADD)
                        if b == 3:
                            if m == CTAPS - 1:
                                i.then_inc(dw_ok, 1)
                            else:
                                dwt.inc(i)

            def pw1_pair(n, lag):
                for j in range(8):
                    lo(G_P1 + 8 * n + j, G_P1 + j)
                    if lag and j == 1:
                        unit(n - 1)
                    if lag and j >= 1:
                        dw(n - 1, order[(j - 1) * 5:j * 5 if j < 7 else CTAPS])
                    if j % 2:
                        ada(176 + 4 * n + j // 2, j // 2 % 2, aring3, aacc3[:, 0, :], 4 * n + j // 2)
            pw1_pair(0, False)
            with dwt.loop(dve, 1, 4, CTAPS - 1) as i:
                pw1_pair(i, True)
            unit(3)
            dw(3, order)
            mod_add(12, 11)
            cw_col(3, 12)
            lv = Tally(ln_v)
            dve.wait_ge(ln_p, 1)
            lv.inc(ts(lnst[:, 0, :], pst[:, 0, :], 1.0 / D, None, MUL))
            lv.wait(dve)
            dve.wait_ge(dw_ok, 4)
            for q in range(4):
                d4 = dwo[:, 4 * q:4 * q + 4, :]
                lv.inc(tt(d4, d4, lnst[:, 0:1, :].broadcast_to([P, 4, T]), SUB))
            dve.wait_ge(ln_p, 5)
            lv.inc(ts(lnst[:, 1, :], pst[:, 2, :], 1.0 / D, LN_EPS, MUL, ADD))
            dve.wait_ge(ln_s, 5)
            lv.inc(nc.vector.reciprocal(lnst[:, 1, :], lnst[:, 1, :]))
            lv.wait(dve)
            for q in range(4):
                d4 = dwo[:, 4 * q:4 * q + 4, :]
                lv.inc(tt(d4, d4, lnst[:, 1:2, :].broadcast_to([P, 4, T]), MUL))
            for j in range(2):
                lo(G_P2 + j, G_P2 + j)
            for q in range(4):
                dve.wait_ge(ln_s, 5 + 2 * (q + 1))
                tt(h_lo3[:, 4 * q:4 * q + 4, :], hf3[:, q % 2], h_hi3[:, 4 * q:4 * q + 4, :].bitcast(F32),
                   SUB).then_inc(pre_lo, 1)
            dve.wait_ge(pb_land, 16)

            def y_bias(n, par):
                dve.wait_ge(w_used, G_P2 + 4 * n + 4)
                for t in range(TT):
                    i = tt(y[:, t, ds(n * NSL, NSL)], psg[:, (S_P2 + par) % 2, t, :], pw2b[:, ds(n * NSL, NSL)], ADD)
                i.then_inc(ps_read, 1)
            lo(G_P2 + 2, G_P2 + 2)
            lo(G_P2 + 3, G_P2 + 3)
            for n in range(1, 4):
                lo(G_P2 + 4 * n, G_P2)
                lo(G_P2 + 4 * n + 1, G_P2 + 1)
                y_bias(n - 1, (n - 1) % 2)
                lo(G_P2 + 4 * n + 2, G_P2 + 2)
                lo(G_P2 + 4 * n + 3, G_P2 + 3)
            y_bias(3, 1)
            post(2, y, cwb)
            pre(3, y, h_hi3, h_lo3, hf3, 12)
            ffn(1, G_F1, S_F1)
            post(3, y, cwb)

        @block.scalar
        def _(act):
            av = nc.scalar.activation

            def hi(g, j):
                act.wait_ge(w_land[j % 4], 4 * (g - j % 4) + 16)
                if not isinstance(g, int) or g >= 2:
                    act.wait_ge(w_used, g - 1)
                av(whi[:, j % 2, :], wraw[:, j % 4, :], ACT.Copy).then_inc(w_hi, 1)

            dump = psg[:, :, :, :].rearrange("p a b n -> p (a b n)")

            def squares(k, src, ready):
                for t in range(TT):
                    act.wait_ge(*ready(t))
                    if k or t:
                        act.wait_ge(sq_ok, TT * k + t)
                    av(dump, src[:, t, :], ACT.Square, accum_out=st[:, k, t:t + 1]).then_inc(sq_ok, 1)
                for t in range(TT):
                    act.wait_ge(ms_ok, TT * k + t + 1)
                    av(st[:, k, t:t + 1], st[:, k, t:t + 1], ACT.Sqrt).then_inc(rt_ok, 1)

            def pre(n, hi_, hfb):
                for q in range(4):
                    act.wait_ge(pre_hf, 4 * n + q + 1)
                    av(hi_[:, 4 * q:4 * q + 4, :], hfb[:, q % 2], ACT.Copy).then_inc(pre_hi, 1)

            act.wait_ge(init, 7)
            act.wait_ge(vec_ok, 1)
            av(cond[:, :], vec[:, NV_C:NV_C + KC], ACT.Silu).then_inc(cond_ok, 1)
            squares(0, x, lambda t: (x_land, 16))
            pre(0, h_hi, hf)
            hi(0, 0)
            hi(1, 1)

            def qk_silu(s):
                act.wait_ge(conv_done, s + 1)
                act.wait_ge(kn_ready, s)
                av(sv[:, :, :], cv[:, qk_silu.par, :, :], ACT.Silu).then_inc(silu_done, 1)
                act.wait_ge(silu_done, s + 1)
                act.wait_ge(nrm_done, s)
                av(sq[:, :, :], sv[:, :, :], ACT.Square).then_inc(l2sq_done, 1)

            def v_silu(s):
                act.wait_ge(conv_done, s + 1)
                act.wait_ge(kn_ready, 8)
                act.wait_ge(vb_done, s - 8)
                av(sv[:, :, :], cv[:, qk_silu.par, :, :], ACT.Silu).then_inc(silu_done, 1)

            def qk_norm(s):
                act.wait_ge(nrm_done, s + 1)
                act.wait_ge(kn_ready, s)
                av(rn[:, :, :], psn[:, :, :], ACT.Ln, bias=epsr[:, 0:1]).then_inc(ln_done, 1)
                act.wait_ge(ln_done, s + 1)
                av(rn[:, :, :], rn[:, :, :], ACT.Exp, scale=-0.5).then_inc(rn_done, 1)

            def v_back(s):
                act.wait_ge(vb_done, s - 7)
                act.wait_ge(kn_out, 16 * s)
                av(kn[:, :, :], psn[:, :, :], ACT.Copy).then_inc(vb_ev, 1)

            def evac(s, par):
                act.wait_ge(w_used, G_QKV + 4 * s + 4)
                act.wait_ge(ps_read, S_QKV + s)
                if not isinstance(s, int) or s >= 2:
                    act.wait_ge(tr_done, s - 1)
                av(ev[:, par, :, :], psg[:, (1 + par) % 2, :, :], ACT.Copy).then_inc(ps_read, 1)

            def z_evac(z, par):
                act.wait_ge(w_used, G_Z + 4 * z + 4)
                act.wait_ge(ps_read, S_Z + z)
                if isinstance(z, int) and z < 2:
                    act.wait_ge(tr_done, 15 + z)
                else:
                    act.wait_ge(zw_done, z - 1)
                av(ev[:, par, :, :], psg[:, (1 + par) % 2, :, :], ACT.Silu).then_inc(ps_read, 1)

            def a_slice(g, g0, first, after0, after1, after3):
                for j in range(4):
                    if j or not first:
                        hi(g + j, g0 + j)
                    for n, f in ((0, after0), (1, after1), (3, after3)):
                        if j == n and f:
                            f()

            def qkv_slice(s, par, kind):
                def a0():
                    qk_silu.par = par
                    (qk_silu if kind == "n" else v_silu)(s - 2)
                a_slice(G_QKV + 4 * s, G_QKV, isinstance(s, int) and s == 0, a0 if kind else None,
                        (lambda: evac(s - 1, 1 - par)) if not (isinstance(s, int) and s == 0) else None,
                        (lambda: (qk_norm if kind == "n" else v_back)(s - 2)) if kind else None)
            qkv_slice(0, 0, None)
            qkv_slice(1, 1, None)
            with act.Fori(0, 4) as i:
                for s in range(2):
                    qkv_slice(2 + 2 * i + s, s, "n")
            with act.Fori(0, 3) as i:
                for s in range(2):
                    qkv_slice(10 + 2 * i + s, s, "v")

            def z_lag(s, par):
                qk_silu.par = par
                v_silu(s)
            a_slice(G_Z, G_Z, False, lambda: z_lag(14, 0), lambda: evac(15, 1), lambda: v_back(14))
            a_slice(G_Z + 4, G_Z, False, lambda: z_lag(15, 1), lambda: z_evac(0, 0), lambda: v_back(15))
            for z in (2, 3):
                a_slice(G_Z + 4 * z, G_Z, False, None, lambda: z_evac(z - 1, 1 - z % 2), None)

            def kk_evac(z):
                act.wait_ge(kk_done, z - 3)
                act.wait_ge(kk_out, 64 * (z - 4))
                blocks = pst[:, :, :].rearrange("p b (t m) -> p b t m", t=TT)
                for q in range(4):
                    r = slice(32 * q, 32 * q + 32)
                    av(kks[r, :, :, :], blocks[r, :, :, r], ACT.Copy).then_inc(kk_ev, 1)
            with act.Fori(2, 4) as i:
                for s in range(2):
                    z = 2 * i + s
                    a_slice(G_Z + 4 * z, G_Z, False, None, lambda: z_evac(z - 1, 1 - s), lambda: kk_evac(z))
            z_evac(7, 1)

            pr = Tally(c_s)
            bt1 = bt[:, 1].rearrange("p a b -> p (a b)")
            act.wait_ge(c_v, 3)
            pr.inc(av(bt1, bt[:, 0].rearrange("p a b -> p (a b)"), ACT.Abs))
            pr.wait(act)
            pr.inc(av(bt1, bt1, ACT.Exp, scale=-1.0))
            pr.wait(act)
            pr.inc(av(bt1, bt1, ACT.Ln, bias=epsr[:, 2:3]))
            pr.inc(av(alog[:, 0, :], alog[:, 0, :], ACT.Exp))
            act.wait_ge(c_v, 4)
            for t in range(TT):
                pr.inc(av(beta[:, t].rearrange("p (d v) h -> p d v h", d=2),
                          bt[:, 2, t, 0:64].rearrange("p (d h v) -> p d v h", d=2, v=2), ACT.Exp))
            act.wait_ge(c_v, C_SUB)
            sflat = sdec[:, :, :, :].rearrange("p c i j -> p (c i j)")
            pr.inc(av(sflat, sflat, ACT.Exp))
            assert pr.n == 7

            act.wait_ge(c_init, C_POOL + 2)
            with act.Fori(0, HQ) as h:
                act.wait_ge(ex_done, h + 1)
                for c in range(4):
                    f = dec[:, c].rearrange("p k s m -> p (k s m)")
                    i = av(f, f, ACT.Exp)
                i.then_inc(dec_done, 1)
                act.wait_ge(w_done, h + 1)
                av(wt[:, :, :, :].rearrange("p c t m -> p (c t) m"), ps_w, ACT.Copy).then_inc(wt_done, 1)
                for o in range(2):
                    act.wait_ge(y_done, 2 * h + o + 1)
                    for d in range(2):
                        q = slice(0, 64) if d == 0 else slice(64, P)
                        av(yh[q, 2 * d:2 * d + 2, :], ps_a[q, 2 * d:2 * d + 2, :], ACT.Copy).then_inc(yc_done, 1)
                    act.wait_ge(u_done, 2 * h + o + 1)
                    av(uu[:, o, :, :], ps_a, ACT.Copy).then_inc(uc_done, 1)
                act.wait_ge(o_done, h + 1)
                act.wait_ge(oms_done, h)
                av(osq[:, :, :], ps_o, ACT.Square).then_inc(osq_done, 1)
                act.wait_ge(oms_done, h + 1)
                act.wait_ge(on_done, h)
                av(oms[:, 1, :], oms[:, 0, :], ACT.Ln, bias=epsr[:, 1:2], scale=1.0 / P).then_inc(oln_done, 1)
                act.wait_ge(oln_done, h + 1)
                av(oms[:, 2, :], oms[:, 1, :], ACT.Exp, scale=-0.5).then_inc(ors_done, 1)
                act.wait_ge(ot_done, h + 1)
                av(oT[:, ds(2 * h, 2), :], ps_oT, ACT.Copy).then_inc(oT_done, 1)

            hi(G_GO, G_GO)
            hi(G_GO + 1, G_GO + 1)
            act.wait_ge(oT_done, HQ)
            for q in range(8):
                av(o_hi[:, 4 * q:4 * q + 4, :], oT[:, 4 * q:4 * q + 4, :], ACT.Copy).then_inc(osp_hi, 1)

            def y_evac(n):
                act.wait_ge(w_used, G_GO + 8 * n + 8)
                av(yg[:, :, n * NSL:(n + 1) * NSL], psg[:, (S_GO + n) % 2, :, :], ACT.Copy).then_inc(ps_read, 1)
            for j in range(2, 8):
                hi(G_GO + j, G_GO + j)
            for n in range(1, 4):
                for j in range(8):
                    hi(G_GO + 8 * n + j, G_GO + j)
                    if j == 1:
                        y_evac(n - 1)
            y_evac(3)
            squares(1, yg, lambda t: (ps_read, S_F0))
            squares(2, x, lambda t: (x_up, t + 1))
            pre(1, h_hi3, hf3)

            def ffn(f, g0, s0):
                nm = GRP * f

                def gate(S, par, g_end):
                    act.wait_ge(w_used, g_end)
                    act.wait_ge(ps_read, S)
                    av(sg[:, :, :], psg[:, (s0 + par) % 2], ACT.Silu).then_inc(ps_read, 1)

                def g_high(n):
                    act.wait_ge(g_tr, nm + n + 1)
                    av(g_hi[:, :, :], pst[:, :, :], ACT.Copy).then_inc(g_hi_ok, 1)
                for j in range(8):
                    if j == 5:
                        gate(s0, 0, g0 + 4)
                    hi(g0 + j, g0 + j)
                with act.Fori(0, (GRP - 1) // 2) as i:
                    for s in range(2):
                        n = 2 * i + s + 1
                        S, g = s0 + 2 + 12 * i + 6 * s, g0 + 8 + 24 * i + 12 * s
                        for j in range(12):
                            if j == 5:
                                gate(S, 0, g + 4)
                            hi(g + j, g0 + j)
                            if j == 2:
                                g_high(n - 1)
                gl = g0 + 8 + 12 * (GRP - 1)
                hi(gl, g0)
                hi(gl + 1, g0 + 1)
                g_high(GRP - 1)
                hi(gl + 2, g0 + 2)
                hi(gl + 3, g0 + 3)

            ffn(0, G_F0, S_F0)
            squares(3, y, lambda t: (ps_read, S_P1))
            squares(4, x, lambda t: (x_up, 3 + t))
            pre(2, h_hi3, hf3)

            def half(n, which):
                act.wait_ge(w_used, G_P1 + 8 * n + 4 * which + 4)
                act.wait_ge(ps_read, S_P1 + 2 * n + which)
                act.wait_ge((t_a, t_g)[which], n)
                av(ev4[:, which, :, :], psg[:, (S_P1 + which) % 2], ACT.Copy).then_inc(ps_read, 1)

            def sigm(n):
                act.wait_ge(t_g, n + 1)
                act.wait_ge(glu_ok, n)
                for b in range(4):
                    i = av(sg4[:, b, :], psn[:, b, :], ACT.Sigmoid, bias=vec[:, ds(V_PW1B + KC + 4 * n + b, 1)])
                i.then_inc(sg_ok, 1)

            def pw1_pair(n, lag):
                for j in range(8):
                    if lag and j == 1:
                        half(n - 1, 1)
                    if j == 5:
                        half(n, 0)
                    hi(G_P1 + 8 * n + j, G_P1 + j)
                    if lag and j == 2:
                        sigm(n - 1)
            pw1_pair(0, False)
            with act.Fori(1, 4) as i:
                pw1_pair(i, True)
            half(3, 1)
            sigm(3)
            hi(G_P2, G_P2)
            hi(G_P2 + 1, G_P2 + 1)
            for q in range(4):
                act.wait_ge(ln_v, 2 + q)
                if q >= 2:
                    act.wait_ge(ln_p, q)
                av(hf3[:, q % 2], dwo[:, 4 * q:4 * q + 4, :], ACT.Square).then_inc(ln_s, 1)
            act.wait_ge(ln_v, 6)
            av(lnst[:, 1, :], lnst[:, 1, :], ACT.Sqrt).then_inc(ln_s, 1)
            for q in range(4):
                act.wait_ge(ln_v, 8 + q)
                if q >= 2:
                    act.wait_ge(pre_lo, 12 + q - 1)
                for j in range(4):
                    kc = 4 * q + j
                    i = av(hf3[:, q % 2, j, :], dwo[:, kc, :], ACT.Silu, bias=vec[:, V_LNB + kc:V_LNB + kc + 1],
                           scale=vec[:, V_LNW + kc:V_LNW + kc + 1])
                i.then_inc(ln_s, 1)
                act.wait_ge(ln_s, 6 + 2 * q)
                av(h_hi3[:, 4 * q:4 * q + 4, :], hf3[:, q % 2], ACT.Copy).then_inc(ln_s, 1)
            for j in range(2, 4):
                hi(G_P2 + j, G_P2 + j)
            with act.Fori(1, 4) as n:
                for j in range(4):
                    hi(G_P2 + 4 * n + j, G_P2 + j)
            squares(5, y, lambda t: (ps_read, S_F1))
            squares(6, x, lambda t: (x_up, 5 + t))
            pre(3, h_hi3, hf3)
            ffn(1, G_F1, S_F1)
            squares(7, y, lambda t: (ps_read, S_F1 + 6 * GRP))

        @block.gpsimd
        def _(pool):
            ms, sel = nc.gpsimd.memset, nc.gpsimd.affine_select
            ms(stage[:, :, :], 0.0).then_inc(init, 1)
            ms(ones[:, :], 1.0).then_inc(init, 1)
            ms(ident[:, :], 0.0).then_inc(init, 1)
            pool.wait_ge(init, 3)
            sel(out=ident[:, :], in_=ident[:, :], compare_op=ALU.not_equal, fill=1.0, base=0,
                pattern=[[-1, P]], channel_multiplier=1).then_inc(init, 1)
            for n, e in enumerate((L2_EPS, RMS_EPS, 1.0)):
                ms(epsr[:, n:n + 1], e).then_inc(init, 1)
            pool.wait_ge(ps_read, 1)
            pool.dma_start(d_ba.rearrange("t p n -> p t n"), ba[:, :, :]).then_inc(ba_out, 16)
            with pool.Fori(0, 8) as s:
                pool.wait_ge(rn_done, s + 1)
                pool.wait_ge(kn_out, 16 * s)
                nc.gpsimd.tensor_tensor(kn[:, :, :], sv[:, :, :], rn[:, :, :], MUL).then_inc(kn_ready, 1)
                pool.wait_ge(kn_ready, s + 1)
                pool.dma_start(d_qkn[ds(4 * s, 4)].rearrange("b p t -> p b t"), kn[:, :, :]).then_inc(kn_out, 16)

            def store_v(s):
                pool.wait_ge(vb_ev, s + 1)
                pool.dma_start(d_v[:, :, ds(s * NSL, NSL)].rearrange("t p n -> p t n"),
                               kn[:, :, :].rearrange("p (t a) b -> p t (a b)", t=TT)).then_inc(kn_out, 16)

            def store_z(z, par):
                pool.wait_ge(ps_read, S_Z + z + 1)
                pool.wait_ge(z_out, 16 * z)
                for t in range(TT):
                    i = nc.gpsimd.tensor_tensor(zw[:, t, :].rearrange("p (a b) -> p a b", b=P),
                                                ev[:, par, t, :].rearrange("p (a b) -> p a b", b=P), gwb[:, :, :], MUL)
                i.then_inc(zw_done, 1)
                pool.wait_ge(zw_done, z + 1)
                pool.dma_start(d_z[:, :, ds(z * NSL, NSL)].rearrange("t p n -> p t n"), zw[:, :, :]).then_inc(z_out, 16)
            with pool.Fori(0, 7) as s:
                store_v(s)
            pool.wait_ge(gw_land, 64)
            store_z(0, 0)
            store_v(7)
            store_z(1, 1)
            store_z(2, 0)
            pool.wait_ge(kn_out, 16 * 16)
            with pool.Fori(2, 4) as i:
                for s in range(2):
                    z = 2 * i + s
                    pool.wait_ge(kk_done, z - 4)
                    pool.dma_start(kst[:, :, :], d_qkn[ds(HQ + 4 * z - 16, 4)].rearrange("b p t -> p b t")).then_inc(kst_land, 16)
                    store_z(z - 1, 1 - s)
                    pool.wait_ge(kk_ev, 4 * (z - 3))
                    dst = d_kk[ds((4 * z - 16) * NBLK, 4 * NBLK)].rearrange("(h t q) i j -> q i h t j", t=TT, q=4)
                    for q in range(4):
                        pool.dma_start(dst[q], kks[32 * q:32 * q + 32, :, :, :]).then_inc(kk_out, 16)
            store_z(7, 1)

            def cw(n, dst, ready):
                pool.wait_ge(cwc_ok, n + 1)
                pool.dma_start(d_cw[n].rearrange("(k p) -> p k", p=P), cwc[:, n, :],
                               allow_slow_non_contiguous=True).then_inc(cw_out, 16)
                pool.wait_ge(cw_out, 16 * (n + 1))
                pool.wait_ge(*ready)
                pool.dma_start(dst[:, :], d_cw[n].partition_broadcast(P)).then_inc(cw_land, 16)

            pr = Tally(c_init)
            pool.wait_ge(c_land, 64)
            for kind, value in ((0, -1.0), (1, float(P) ** -0.5)):
                pr.inc(ms(masks[:, :, kind], value))
            pr.wait(pool)
            for d in range(2):
                for kind in range(2):
                    for seg in (0, 2):
                        m, sign = masks[:, d, kind, seg, :], 1 - 2 * d
                        pr.inc(sel(out=m, in_=m, compare_op=ALU.is_gt if kind == 0 else ALU.is_ge, fill=0.0, base=0,
                                   pattern=[[sign, P]], channel_multiplier=-sign))
            pr.inc(ms(tri[:, :, :], 1.0))
            pr.wait(pool)
            for n, (sign, op) in enumerate(((1, ALU.is_ge), (-1, ALU.is_gt), (-1, ALU.is_ge), (1, ALU.is_gt))):
                pr.inc(sel(out=tri[:, n, :], in_=tri[:, n, :], compare_op=op, fill=0.0, base=0,
                           pattern=[[sign, P]], channel_multiplier=-sign))
            pr.inc(ms(m64[:, :, :], 0.0))
            pr.wait(pool)
            for d in range(2):
                for b in (0, 64):
                    r = b + 32 * d
                    pr.inc(ms(m64[r:r + 32, d, b + 32 - 32 * d:b + 64 - 32 * d], 1.0))
                    pr.wait(pool)
            pr.inc(ms(sinv[:, 0], 0.0))
            pr.wait(pool)
            pr.inc(ms(sinv[:, 0].rearrange("p c i j -> p c (i j)")[:, :, 0:1024:33], 1.0))
            assert pr.n == C_POOL
            pool.wait_ge(inv_out, 16)
            pr.inc(ms(inv[:, :, :, :, :], 0.0))
            pr.inc(ms(yh[:, :, :], 0.0))

            with pool.Fori(0, HQ) as h:
                pool.wait_ge(v_land, 16 * (h + 1))
                pool.wait_ge(uc_done, 2 * h)
                for o in range(2):
                    for d in range(2):
                        t = o if d == 0 else 1 - o
                        nc.gpsimd.tensor_tensor(rv[:, o, 2 * d:2 * d + 2, :], vt[:, t, :, :],
                                                beta[:, t, 2 * d:2 * d + 2, ds(h, 1)].broadcast_to([P, 2, P]),
                                                MUL).then_inc(rv_done, 1)
            cw(0, cwb0, (oT_done, HQ))
            cw(1, cwb, (x_up, 2))
            cw(2, cwb, (x_up, 4))
            cw(3, cwb, (x_up, 6))


_INS = ["x", "c", "ada_w", "ada_b", "norm_w", "gdn_in_w", "gdn_conv_w", "gdn_A_log", "gdn_dt_bias", "gdn_norm_w",
        "gdn_out_w", "cf_pw1_w", "cf_pw1_b", "cf_dw_w", "cf_dw_b", "cf_ln_w", "cf_ln_b", "cf_pw2_w", "cf_pw2_b",
        "ffn_in_w", "ffn_out_w"]


def kernel(**inputs):
    import numpy as np
    import concourse.bacc as bacc
    from concourse.bass_utils import run_bass_kernel_spmd

    nc = bacc.Bacc("TRN2", target_bir_lowering=False, num_devices=1)
    arrays, args = {}, []
    for name in _INS:
        a = np.ascontiguousarray(inputs[name])
        arrays["in_" + name] = a
        args.append(nc.dram_tensor("in_" + name, a.shape, mybir.dt.from_np(a.dtype), kind="ExternalInput").ap())
    shape = tuple(inputs["x"].shape)
    args.append(nc.dram_tensor("out_x", shape, mybir.dt.float32, kind="ExternalOutput").ap())
    build(nc, *args)
    r = run_bass_kernel_spmd(nc, [arrays], core_ids=[0])
    return r.results[0]["out_x"]
```

```python
import concourse.bass as bass
from concourse import mybir
from contextlib import ExitStack, contextmanager

P = 128
D = 2048
T = 256
TT = T // P
KC = D // P
NSL = 512
KT = 4
TILE = KT * NSL
HQ, HV = 16, 32
QKV = 2 * HQ * P + HV * P
NQKV = QKV // NSL
VD = HV * P
NZ = VD // NSL
TAPS = 5
CTAPS = 31
TAPS_S = tuple(range(6)) + tuple(range(CTAPS - 6, CTAPS))
TAPS_V = (CTAPS // 2,) + tuple(k for k in range(6, CTAPS - 6) if k != CTAPS // 2)
HID = 5632
GRP = HID // NSL
ADA_AT = (0, 1, 2, 3, 4, 5, 8, 10, 11)
NBLK = T // 32
RMS_EPS, LN_EPS, L2_EPS = 1e-6, 1e-5, 1e-6


class Tally:

    def __init__(self, sem, n=0):
        self.sem, self.n, self.off = sem, n, 0

    def inc(self, instruction):
        instruction.then_inc(self.sem, 1)
        self.n += 1

    def at(self):
        return self.n + self.off

    def wait(self, engine):
        engine.wait_ge(self.sem, self.at())

    @contextmanager
    def loop(self, engine, start, end, per):
        n0 = self.n
        with engine.Fori(start, end) as i:
            self.off = (i - start) * per
            yield i
        assert self.n == n0 + per
        self.n, self.off = n0 + per * (end - start), 0


def build(nc, x_in, c_in, ada_w, ada_b, norm_w, gdn_in_w, gdn_conv_w, gdn_A_log, gdn_dt_bias,
          gdn_norm_w, gdn_out_w, cf_pw1_w, cf_pw1_b, cf_dw_w, cf_dw_b, cf_ln_w, cf_ln_b,
          cf_pw2_w, cf_pw2_b, ffn_in_w, ffn_out_w, out):
    F32, F32R = mybir.dt.float32, mybir.dt.float32r
    ALU = mybir.AluOpType
    ACT = mybir.ActivationFunctionType
    AX = mybir.AxisListType.X
    ds = bass.ds
    MUL, ADD, SUB, MIN = ALU.mult, ALU.add, ALU.subtract, ALU.min

    G_BA = 0
    G_QKV = 1
    G_Z = G_QKV + 4 * NQKV
    G_GO = G_Z + 4 * NZ
    G_F0 = G_GO + 8 * 4
    G_P1 = G_F0 + 12 * GRP
    G_P2 = G_P1 + 4 * 8
    G_F1 = G_P2 + 4 * 4
    S_QKV = 1
    S_Z = S_QKV + NQKV
    S_GO = S_Z + NZ
    S_F0 = S_GO + 4
    S_P1 = S_F0 + 6 * GRP
    S_P2 = S_P1 + 8
    S_F1 = S_P2 + 4

    stack = ExitStack()
    with stack:
        def sb(name, shape, dt=F32, at=stack):
            return at.enter_context(nc.sbuf_tensor(name, shape, dt))

        def sem(name):
            return stack.enter_context(nc.semaphore(name))

        def dram(name, shape):
            return nc.dram_tensor(name, shape, F32, kind="Internal").ap()

        d_qkn = dram("d_qkn", (2 * HQ, P, T))
        d_v = dram("d_v", (TT, P, VD))
        d_z = dram("d_z", (TT, P, VD))
        d_rows = dram("d_rows", (8 * HQ, T))
        d_kk = dram("d_kk", (HQ * NBLK, 32, 32))
        d_inv = dram("d_inv", (HQ * NBLK, 2, 4, 32, 32))
        d_ba = dram("d_ba", (TT, P, P))
        d_cw = dram("d_cw", (4, D))

        x = sb("x", [P, TT, D])
        wraw = sb("wraw", [P, 4, TILE])
        whi = sb("whi", [P, 2, TILE], F32R)
        wlo = sb("wlo", [P, 2, TILE], F32R)
        ident = sb("ident", [P, P])
        ones = sb("ones", [P, P])
        NV_NORM, NV_ADAB, NV_C, NV_CONV, NV_DW, NV_CF = 0, 128, 320, 336, 656, 1152
        vec = sb("vec", [P, 1232])
        V_PW1B, V_DWB, V_LNW, V_LNB = NV_CF, NV_CF + 32, NV_CF + 48, NV_CF + 64
        cond = sb("cond", [P, KC])
        mod = sb("mod", [P, 12, KC])
        aff = sb("aff", [P, 4, KC])
        cwc = sb("cwc", [P, 4, KC])
        st = sb("st", [P, 8, TT])
        spart = sb("spart", [P, TT, 4])
        epsr = sb("epsr", [P, 3])

        ada_st = ExitStack()
        aring = sb("aring", [P, 2, D], at=ada_st)
        aacc = sb("aacc", [P, 2, D], at=ada_st)
        p1 = ExitStack()
        p0 = ExitStack()
        aring0 = sb("aring0", [P, 4, D], at=p0)
        p0.close()
        h_hi = sb("h_hi", [P, KC, T], F32R, at=p1)
        h_lo = sb("h_lo", [P, KC, T], F32R, at=p1)
        hf = sb("hf", [P, 2, 4, T], at=p1)
        p1a = ExitStack()
        stage = sb("stage", [P, 12, P], at=p1a)
        y1 = sb("y1", [P, TT, D], at=p1a)
        p1a.close()
        ev = sb("ev", [P, 2, TT, NSL], at=p1)
        cv = sb("cv", [P, 2, 4, T], at=p1)
        sv = sb("sv", [P, 4, T], at=p1)
        sq = sb("sq", [P, 4, T], at=p1)
        rn = sb("rn", [P, 4, T], at=p1)
        kn = sb("kn", [P, 4, T], at=p1)
        kst = sb("kst", [P, 4, T], at=p1)
        zw = sb("zw", [P, TT, NSL], at=p1)
        kks = sb("kks", [P, 4, TT, 32], at=p1)
        ba = sb("ba", [P, TT, P], at=p1)
        gwb = sb("gwb", [P, 4, P], at=p1)
        p1.close()
        ada_st.close()
        p2 = ExitStack()
        oT = sb("oT", [P, HV, T], at=p2)
        p2a = ExitStack()
        ncum = sb("ncum", [P, 2, TT, 4, HQ], at=p2a)
        beta = sb("beta", [P, TT, 4, HQ], at=p2a)
        masks = sb("masks", [P, 2, 2, 3, P], at=p2a)
        m64 = sb("m64", [P, 2, P], at=p2a)
        tri = sb("tri", [P, 4, P], at=p2a)
        epoch = ExitStack()
        ba2 = sb("ba2", [P, TT, P], at=epoch)
        bt = sb("bt", [P, 3, TT, P], at=epoch)
        alog = sb("alog", [P, 2, 64], at=epoch)
        rowsT = sb("rowsT", [P, TT, P], at=epoch)
        rows = sb("rows", [P, T], at=epoch)
        skk = sb("skk", [P, 32, 32], at=epoch)
        srow = sb("srow", [P, 8, 32], at=epoch)
        sdec = sb("sdec", [P, 4, 32, 32], at=epoch)
        stmp = sb("stmp", [P, 2, 2, 256], at=epoch)
        sinv = sb("sinv", [P, 2, 4, 32, 32], at=epoch)
        epoch.close()
        qk = sb("qk", [P, 2, T], at=p2a)
        rr = sb("rr", [P, 8, T], at=p2a)
        vt = sb("vt", [P, TT, 2, P], at=p2a)
        zt = sb("zt", [P, TT, 2, P], at=p2a)
        inv = sb("inv", [P, 2, 4, TT, P], at=p2a)
        mk = sb("mk", [P, 2, 2, 3, P], at=p2a)
        dec = sb("dec", [P, 2, 4, 2, 3, P], at=p2a)
        lm = sb("lm", [P, 4, TT, P], at=p2a)
        free_slot = wraw[:, (G_GO + 3) % 4, :].rearrange("p (a b c m) -> p a b c m", a=2, b=4, c=TT)
        wt = free_slot[:, 0]
        exb = wraw[:, (G_GO + 1) % 4:(G_GO + 1) % 4 + 2, :].rearrange("p a n -> p (a n)")[:, 0:24 * P].rearrange(
            "p (c k s m) -> p c k s m", c=4, k=2, s=3)
        assert (G_GO + 1) % 4 == 2 and (G_GO + 3) % 4 == 0
        uu = free_slot[:, 1].rearrange("p b c m -> p (b c m)").rearrange("p (o c m) -> p o c m", o=2, c=4)
        t64 = sb("t64", [P, 2, 4, TT, P], at=p2a)
        rv = sb("rv", [P, 2, 2, 4, P], at=p2a)
        yh = sb("yh", [P, 4, P], at=p2a)
        osq = sb("osq", [P, 4, P], at=p2a)
        og = sb("og", [P, 4, P], at=p2a)
        oms = sb("oms", [P, 3, 4], at=p2a)
        p2a.close()
        o_hi = sb("o_hi", [P, HV, T], F32R, at=p2)
        o_lo = sb("o_lo", [P, HV, T], F32R, at=p2)
        yg = sb("yg", [P, TT, D], at=p2)
        cwb0 = sb("cwb0", [P, D], at=p2)
        dump0 = oT[:, 0:2, :].rearrange("p a t -> p (a t)")
        p2.close()
        p3 = ExitStack()
        aring3 = sb("aring3", [P, 2, D], at=p3)
        aacc3 = sb("aacc3", [P, 2, D], at=p3)
        h_hi3 = sb("h_hi3", [P, KC, T], F32R, at=p3)
        h_lo3 = sb("h_lo3", [P, KC, T], F32R, at=p3)
        hf3 = sb("hf3", [P, 2, 4, T], at=p3)
        y = sb("y", [P, TT, D], at=p3)
        cwb = sb("cwb", [P, D], at=p3)
        p3a = ExitStack()
        sg = sb("sg", [P, TT, NSL], at=p3a)
        gg = sb("gg", [P, TT, NSL], at=p3a)
        g_hi = sb("g_hi", [P, 4, T], F32R, at=p3a)
        g_lo = sb("g_lo", [P, 4, T], F32R, at=p3a)
        p3a.close()
        p4 = ExitStack()
        ev4 = sb("ev4", [P, 2, TT, NSL], at=p4)
        lnst = sb("lnst", [P, 2, T], at=p4)
        sg4 = sb("sg4", [P, 4, T], at=p4)
        glu = sb("glu", [P, 4, T], at=p4)
        p4.close()
        p3.close()
        dwp = aring3[:, :, :].rearrange("p a (c b t) -> p (a c) b t", c=2, b=4)
        dwa = aacc3[:, 0, 0:4 * T].rearrange("p (b t) -> p b t", b=4)
        pw2b = ev4[:, :, :, :].rearrange("p a t n -> p (a t n)")
        dwo = y[:, :, :].rearrange("p a (k t) -> p (a k) t", t=T)

        psg = stack.enter_context(nc.psum_tensor("psg", [P, 2, TT, NSL], F32))
        pst = stack.enter_context(nc.psum_tensor("pst", [P, 4, T], F32))
        psn = stack.enter_context(nc.psum_tensor("psn", [P, 4, T], F32))

        ps_w = psg[:, 1, :, :].rearrange("p a (b m) -> p (a b) m", m=P)
        ps_a = pst[:, 0:2, :].rearrange("p a (b m) -> p (a b) m", m=P)
        ps_b = pst[:, 2:4, :].rearrange("p a (b m) -> p (a b) m", m=P)
        ps_o = psn[:, 0:2, :].rearrange("p a (b m) -> p (a b) m", m=P)
        ps_oT = psn[:, 2:4, :]

        w_land = [sem(f"w_land{i}") for i in range(4)]
        w_hi = sem("w_hi")
        w_lo = sem("w_lo")
        w_used = sem("w_used")
        ps_read = sem("ps_read")
        a_land = [sem(f"a_land{i}") for i in range(2)]
        a0_land = [sem(f"a0_land{i}") for i in range(4)]
        a_zero = sem("a_zero")
        a_used = sem("a_used")
        a_fin = sem("a_fin")
        mod_ok = sem("mod_ok")
        init = sem("init")
        vec_land = sem("vec_land")
        x_land = sem("x_land")
        vec_tr = sem("vec_tr")
        vec_ok = sem("vec_ok")
        cond_ok = sem("cond_ok")
        sq_ok = sem("sq_ok")
        ms_ok = sem("ms_ok")
        rt_ok = sem("rt_ok")
        rs_ok = sem("rs_ok")
        xn_ok = sem("xn_ok")
        pre_tr = sem("pre_tr")
        hf_v, hf_s = sem("hf_v"), sem("hf_s")
        pre_hi = sem("pre_hi")
        pre_lo = sem("pre_lo")
        aff_ok = sem("aff_ok")
        x_up = sem("x_up")
        yq_ok = sem("yq_ok")
        yr_ok = sem("yr_ok")
        yrt_ok = sem("yrt_ok")
        yc_ok = sem("yc_ok")
        tr_done = sem("tr_done")
        conv_done = sem("conv_done")
        tap = sem("tap")
        silu_done = sem("silu_done")
        l2sq_done = sem("l2sq_done")
        nrm_done = sem("nrm_done")
        ln_done = sem("ln_done")
        rn_done = sem("rn_done")
        kn_ready = sem("kn_ready")
        kn_out = sem("kn_out")
        vb_done = sem("vb_done")
        vb_ev = sem("vb_ev")
        zw_done = sem("zw_done")
        z_out = sem("z_out")
        kst_land = sem("kst_land")
        kk_done = sem("kk_done")
        kk_ev = sem("kk_ev")
        kk_out = sem("kk_out")
        ba_out = sem("ba_out")
        cwc_ok = sem("cwc_ok")
        cw_out = sem("cw_out")
        cw_land = sem("cw_land")
        gw_land = sem("gw_land")
        c_land = sem("c_land")
        c_init = sem("c_init")
        c_v = sem("c_v")
        c_s = sem("c_s")
        c_p = sem("c_p")
        rows_out = sem("rows_out")
        s_land = sem("s_land")
        inv_out = sem("inv_out")
        qk_land, rr_land, v_land, z_land, inv_land = (sem(n) for n in ("qk_land", "rr_land", "v_land", "z_land", "inv_land"))
        kq_done = sem("kq_done")
        mk_done = sem("mk_done")
        ex_done = sem("ex_done")
        d0_done, d1_done = sem("d0_done"), sem("d1_done")
        la_done = sem("la_done")
        aq_done = sem("aq_done")
        lm_done = sem("lm_done")
        w_done, wt_done, t_done, t64_done = (sem(n) for n in ("w_done", "wt_done", "t_done", "t64_done"))
        rv_done = sem("rv_done")
        y_done, yc_done, h_done, s_done, u_done, uc_done = (sem(n) for n in ("y_done", "yc_done", "h_done", "s_done", "u_done", "uc_done"))
        x_done, r2_done = sem("x_done"), sem("r2_done")
        o_done, osq_done, oms_done, oln_done, ors_done, on_done, og_done, ot_done, oT_done = (
            sem(n) for n in ("o_done", "osq_done", "oms_done", "oln_done", "ors_done", "on_done", "og_done", "ot_done", "oT_done"))
        osp_hi, osp_lo = sem("osp_hi"), sem("osp_lo")
        g_tr, g_hi_ok, g_lo_ok, y_zero = (sem(n) for n in ("g_tr", "g_hi_ok", "g_lo_ok", "y_zero"))
        dwp_ok, dwa_ok = sem("dwp_ok"), sem("dwa_ok")
        t_a, t_g, sg_ok, glu_ok, dw_ok = (sem(n) for n in ("t_a", "t_g", "sg_ok", "glu_ok", "dw_ok"))
        ln_p, ln_v, ln_s = sem("ln_p"), sem("ln_v"), sem("ln_s")
        pb_land = sem("pb_land")
        out_sem = sem("out_sem")

        C_G, C_ROWT, C_ROWS, C_SUB, C_DEC = 5, 13, 14, 17, 21
        C_INV = C_DEC + 2 * (2 * 31 + 1)
        C_POOL = 22
        C_POOL_INV = C_POOL + 2 * 31 + 1

        block = stack.enter_context(nc.Block())

        def invert(engine, ops, count, parts):
            for n in range(31):
                steps = []
                for d, v0, v1 in parts:
                    j, a, b = (n, n + 1, 32) if d == 0 else (31 - n, 0, 31 - n)
                    c0, c1 = (0, j + 1) if d == 0 else (j, 32)
                    shape = [P, v1 - v0, b - a, c1 - c0]
                    tmp = stmp[:, d, v0:v1, 0:(b - a) * (c1 - c0)].rearrange("p v (i c) -> p v i c", c=c1 - c0)
                    steps.append((tmp, slice(2 * d + v0, 2 * d + v1), j, a, b, c0, c1, shape))
                count.wait(engine)
                for tmp, c, j, a, b, c0, c1, shape in steps:
                    count.inc(ops.tensor_tensor(tmp, sdec[:, c, a:b, j].unsqueeze(3).broadcast_to(shape),
                                                sinv[:, 0, c, j, c0:c1].unsqueeze(2).broadcast_to(shape), MUL))
                count.wait(engine)
                for tmp, c, j, a, b, c0, c1, shape in steps:
                    to = sinv[:, 0, c, a:b, c0:c1]
                    count.inc(ops.tensor_tensor(to, to, tmp, ADD))
            count.wait(engine)
            for _, c, *_ in steps:
                count.inc(ops.tensor_copy(sinv[:, 1, c].rearrange("p c i j -> p c j i"), sinv[:, 0, c]))

        def rows4(w, r0, n0):
            return w[ds(r0, KT * P), ds(n0, NSL)].rearrange("(j p) n -> p j n", p=P)

        def tile4(ap):
            return ap.rearrange("p (j n) -> p j n", n=NSL)

        gdn_in, gdn_out = gdn_in_w[0], gdn_out_w[0]
        pw1, pw2 = cf_pw1_w[0], cf_pw2_w[0]

        @block.sync
        def _(sp):
            def load_w(g, slot, src, dst=None):
                if not isinstance(g, int) or g >= 4:
                    sp.wait_ge(w_lo, g - 3)
                sp.dma_start(tile4(wraw[:, slot, :]) if dst is None else dst, src).then_inc(w_land[slot], 16)

            def load_ada(a, ring, flat, k):
                layer, part = flat
                slot = load_ada.slot
                load_ada.slot = 1 - slot
                if not isinstance(a, int) or a >= 2:
                    sp.wait_ge(a_used, a - 1)
                sp.dma_start(ring[:, slot, :], ada_w[layer][ds(k * P, P), ds(part * D, D)]).then_inc(a_land[slot], 16)
            load_ada.slot = 0

            def load_ada0(a):
                if a >= 4:
                    sp.wait_ge(a_used, a - 3)
                sp.dma_start(aring0[:, a % 4, :], ada_w[0][a % KC * P:(a % KC + 1) * P, a // KC * D:(a // KC + 1) * D]
                             ).then_inc(a0_land[a % 4], 16)

            sp.wait_ge(init, 1)
            for r0, src in ((0, norm_w.rearrange("l n (k p) -> (l n k) p", p=P)),
                            (1, ada_b[0:1].rearrange("a (k p) -> (a k) p", p=P)),
                            (2, ada_b[1:2].rearrange("a (k p) -> (a k) p", p=P)),
                            (3, c_in.rearrange("a (k p) -> (a k) p", p=P))):
                sp.dma_start(stage[0:src.shape[0], r0, :], src).then_inc(vec_land, 16)
            sp.dma_start(x[:, :, :], x_in[0].rearrange("(t p) d -> p t d", p=P)).then_inc(x_land, 16)
            conv_rows = gdn_conv_w[0].rearrange("k (b p) -> (k b) p", p=P)
            for n in range(3):
                r = min(P, conv_rows.shape[0] - n * P)
                sp.dma_start(stage[0:r, 4 + n, :], conv_rows[n * P:n * P + r, :]).then_inc(vec_land, 16)
            dw_rows = cf_dw_w[0].rearrange("k (b p) -> (k b) p", p=P)
            for n in range(4):
                r = min(P, dw_rows.shape[0] - n * P)
                sp.dma_start(stage[0:r, 7 + n, :], dw_rows[n * P:n * P + r, :]).then_inc(vec_land, 16)
            r0 = 0
            for src in (cf_pw1_b, cf_dw_b, cf_ln_w, cf_ln_b):
                s = src.rearrange("a (k p) -> (a k) p", p=P)
                sp.dma_start(stage[r0:r0 + s.shape[0], 11, :], s).then_inc(vec_land, 16)
                r0 += s.shape[0]
            for j in range(4):
                sp.dma_start(gwb[:, j, :], gdn_norm_w[0].partition_broadcast(P)).then_inc(gw_land, 16)
            for a in range(4):
                load_ada0(a)
            load_w(G_BA, 0, gdn_in[:, QKV + VD:QKV + VD + P].rearrange("(j p) n -> p j n", p=P),
                   wraw[:, 0, :].rearrange("p (j n) -> p j n", n=P))
            for a in range(4, 2 * KC):
                load_ada0(a)
            def load_qkv(s):
                for j in range(4):
                    load_w(G_QKV + 4 * s + j, (G_QKV + j) % 4, rows4(gdn_in, j * KT * P, s * NSL))
                    if j == 2:
                        load_ada(32 + s, aring, (0, 2), s)
            load_qkv(0)
            load_qkv(1)
            with sp.Fori(0, NQKV // 2 - 1) as i:
                for s in range(2):
                    load_qkv(2 * i + s + 2)
            for part, z0 in ((3, 0), (4, 4)):
                with sp.Fori(0, 2) as i:
                    for s in range(2):
                        for j in range(4):
                            zs = z0 + 2 * i + s
                            load_w(G_Z + 4 * zs + j, (G_Z + j) % 4, rows4(gdn_in, j * KT * P, QKV + zs * NSL))
                            load_ada(48 + 4 * zs + j, aring, (0, part), 8 * i + 4 * s + j)
            load_w(G_GO, G_GO % 4, rows4(gdn_out, 0, 0))
            sp.wait_ge(w_used, G_GO)
            sp.wait_ge(ps_read, S_GO)
            sp.wait_ge(z_out, 16 * NZ)
            sp.wait_ge(kk_out, 16 * 4 * 4)
            sp.wait_ge(vb_ev, 8)
            sp.wait_ge(kn_out, 16 * 16)
            sp.wait_ge(mod_ok, 5)
            sp.wait_ge(ba_out, 16)
            sp.dma_start(ba2[:, :, :], d_ba.rearrange("t p n -> p t n")).then_inc(c_land, 16)
            sp.dma_start(alog[:, 0, :], gdn_A_log[0].rearrange("a b -> (a b)").partition_broadcast(P)).then_inc(c_land, 16)
            sp.dma_start(alog[:, 1, :], gdn_dt_bias[0].rearrange("a b -> (a b)").partition_broadcast(P)).then_inc(c_land, 16)
            sp.dma_start(skk[:, :, :].rearrange("p a b -> p (a b)"), d_kk.rearrange("p a b -> p (a b)")).then_inc(c_land, 16)
            sp.wait_ge(c_v, C_ROWS)
            sp.dma_start(d_rows, rows[:, :]).then_inc(rows_out, 16)
            sp.wait_ge(rows_out, 16)
            sp.dma_start(srow[:, :, :], d_rows.rearrange("(c h) (b i) -> (h b) c i", h=HQ, i=32)).then_inc(s_land, 16)
            sp.wait_ge(c_v, C_INV)
            sp.wait_ge(c_init, C_POOL_INV)
            sp.dma_start(d_inv.rearrange("p a c i j -> p (a c i j)"),
                         sinv[:, :, :, :, :].rearrange("p a c i j -> p (a c i j)")).then_inc(inv_out, 16)
            sp.wait_ge(inv_out, 16)
            sp.wait_ge(c_init, C_POOL_INV + 1)
            inv_view = d_inv.rearrange("(h t q) a c i j -> h t q i (a c) j", t=TT, q=4)

            def load_qk(h):
                sp.dma_start(qk[:, 0, :], d_qkn[ds(HQ + h, 1)].rearrange("a p t -> p (a t)")).then_inc(qk_land, 16)
                sp.dma_start(qk[:, 1, :], d_qkn[ds(h, 1)].rearrange("a p t -> p (a t)")).then_inc(qk_land, 16)

            def load_rr(h):
                sp.dma_start(rr[:, :, :], d_rows.rearrange("(c h) t -> h c t", h=HQ)[ds(h, 1)].rearrange(
                    "a c t -> (a c) t").partition_broadcast(P)).then_inc(rr_land, 16)

            def load_v(h):
                sp.dma_start(vt[:, :, :, :].rearrange("p t a m -> p t (a m)"),
                             d_v[:, :, ds(2 * P * h, 2 * P)].rearrange("t p n -> p t n")).then_inc(v_land, 16)

            def load_z(h):
                sp.dma_start(zt[:, :, :, :].rearrange("p t a m -> p t (a m)"),
                             d_z[:, :, ds(2 * P * h, 2 * P)].rearrange("t p n -> p t n")).then_inc(z_land, 16)

            def load_inv(h):
                for t in range(TT):
                    for q in range(4):
                        sp.dma_start(inv[32 * q:32 * q + 32, :, :, t, 32 * q:32 * q + 32].rearrange("p a c j -> p (a c) j"),
                                     inv_view[ds(h, 1), t, q].rearrange("a i c j -> (a i) c j")).then_inc(inv_land, 16)

            def core_loads(h, nxt=True, z=True, r=True):
                if r:
                    sp.wait_ge(kq_done, h + 2)
                    load_qk(h + 2)
                if nxt:
                    sp.wait_ge(rv_done, 4 * (h + 1))
                    load_v(h + 1)
                    sp.wait_ge(t64_done, h + 1)
                    load_inv(h + 1)
                if z:
                    if not isinstance(h, int) or h > 1:
                        sp.wait_ge(og_done, h - 1)
                    load_z(h - 1)
                if r:
                    sp.wait_ge(ex_done, h + 2)
                    load_rr(h + 2)
            load_rr(0)
            load_qk(0)
            core_loads(-1, z=False)
            core_loads(0, z=False)
            core_loads(1)
            with sp.Fori(2, HQ - 2) as h:
                core_loads(h)
            core_loads(HQ - 2, r=False)
            core_loads(HQ - 1, nxt=False, r=False)
            core_loads(HQ, nxt=False, r=False)
            sp.wait_ge(oT_done, HQ)
            for j in range(1, 8):
                load_w(G_GO + j, (G_GO + j) % 4, rows4(gdn_out, j * KT * P, 0))
            with sp.Fori(1, 4) as n:
                for j in range(8):
                    load_w(G_GO + 8 * n + j, (G_GO + j) % 4, rows4(gdn_out, j * KT * P, n * NSL))

            def load_ffn(layer, g0):
                w_in, w_out, a0 = ffn_in_w[layer], ffn_out_w[layer], (80, 176)[layer]
                for j in range(8):
                    if j == 4:
                        sp.wait_ge(x_up, 2 + 4 * layer)
                        load_ada(a0, aring3, (layer, 5), 0)
                        load_ada(a0 + 1, aring3, (layer, 5), 1)
                    load_w(g0 + j, (g0 + j) % 4, rows4(w_in, (j % 4) * KT * P, (j // 4) * HID))
                    if j >= 4:
                        load_ada(a0 + j - 2, aring3, (layer, 5), j - 2)
                with sp.Fori(0, (GRP - 1) // 2) as i:
                    at = 0
                    for s in range(2):
                        n = 2 * i + s + 1
                        for j in range(12):
                            if j < 4:
                                src = rows4(w_in, j * KT * P, n * NSL)
                            elif j < 8:
                                src = rows4(w_out, (n - 1) * NSL, (j - 4) * NSL)
                            else:
                                src = rows4(w_in, (j - 8) * KT * P, HID + n * NSL)
                            load_w(g0 + 8 + 24 * i + 12 * s + j, (g0 + j) % 4, src)
                            if layer and j == 6:
                                load_ada(a0 + 6 + 2 * i + s, aring3, (1, 5), 6 + 2 * i + s)
                            if layer == 0 and j in ADA_AT:
                                flat, k = ((1, i), at) if at < 16 else ((0, 5), 6 + 2 * i + at - 16)
                                load_ada(86 + 18 * i + at, aring3, flat, k)
                                at += 1
                for j in range(4):
                    g = g0 + 8 + 12 * (GRP - 1) + j
                    load_w(g, g % 4, rows4(w_out, (GRP - 1) * NSL, j * NSL))

            load_ffn(0, G_F0)
            with sp.Fori(0, 4) as i:
                for j in range(8):
                    load_w(G_P1 + 8 * i + j, (G_P1 + j) % 4, rows4(pw1, (j % 4) * KT * P, i * NSL + (j // 4) * D))
            for j in range(4):
                load_w(G_P2 + j, (G_P2 + j) % 4, rows4(pw2, j * KT * P, 0))
            sp.wait_ge(t_g, 4)
            sp.wait_ge(t_a, 4)
            sp.dma_start(pw2b, cf_pw2_b[0].partition_broadcast(P)).then_inc(pb_land, 16)
            with sp.Fori(1, 4) as n:
                for j in range(4):
                    load_w(G_P2 + 4 * n + j, (G_P2 + j) % 4, rows4(pw2, j * KT * P, n * NSL))
            load_ffn(1, G_F1)
            for t in range(TT):
                sp.wait_ge(x_up, 7 + t)
                sp.dma_start(out[0, t * P:(t + 1) * P, :], x[:, t, :]).then_inc(out_sem, 16)
            sp.wait_ge(out_sem, 16 * TT)

        @block.tensor
        def _(pe):
            mm = nc.tensor.matmul

            def tr(dst, src):
                return nc.tensor.transpose(dst, src, ident[:, :])

            def tile(g, slot, ps, a_hi, a_lo, kcs, first, last, width=NSL, ready=None):
                pe.wait_ge(w_lo, g + 1)
                if ready:
                    pe.wait_ge(*ready)
                for j, kc in enumerate(kcs):
                    for t in range(TT):
                        o = ps[:, t, 0:width]
                        ah, al = a_hi[:, kc, t * P:(t + 1) * P], a_lo[:, kc, t * P:(t + 1) * P]
                        wh, wl = (w[:, slot, j * width:(j + 1) * width] for w in (whi, wlo))
                        mm(o, ah, wh, start=first and j == 0, stop=False)
                        mm(o, ah, wl, start=False, stop=False)
                        i = mm(o, al, wh, start=False, stop=last and j == len(kcs) - 1)
                i.then_inc(w_used, 1)

            def pre(n, src):
                for q in range(4):
                    if q == 0:
                        pe.wait_ge(xn_ok, TT * (n + 1))
                    if q >= 2:
                        pe.wait_ge((hf_v, hf_s)[q % 2], 2 * n + 1)
                    ps = (pst, psn)[q % 2]
                    for j in range(4):
                        for t in range(TT):
                            i = tr(ps[:, j, t * P:(t + 1) * P], src[:, t, (4 * q + j) * P:(4 * q + j + 1) * P])
                    i.then_inc(pre_tr, 1)

            def fin(a_end, acc):
                pe.wait_ge(a_used, a_end)
                for kc in range(KC):
                    i = mm(psn[:, 0, kc:kc + 1], acc[:, kc * P:(kc + 1) * P], ones[:, 0:1], start=True, stop=True)
                i.then_inc(a_fin, 1)

            pe.wait_ge(init, 4)
            pe.wait_ge(vec_land, 16 * 15)
            vps = psg[:, :, :, :].rearrange("p a b n -> p (a b n)")
            for n in range(12):
                i = tr(vps[:, n * P:(n + 1) * P], stage[:, n, :])
            i.then_inc(vec_tr, 1)
            fin(16, aacc[:, 0, :])
            pe.wait_ge(mod_ok, 1)
            fin(32, aacc[:, 1, :])
            pe.wait_ge(mod_ok, 2)
            pe.wait_ge(vec_ok, 1)
            pre(0, y1)
            pe.wait_ge(pre_lo, 4)
            pe.wait_ge(sq_ok, 2)
            tile(G_BA, 0, psg[:, 0], h_hi, h_lo, range(KC), True, True, width=P)

            def qkv_slice(s, par, lag1, lag2):
                S = S_QKV + s
                for j in range(4):
                    if j == 0 and (not isinstance(S, int) or S >= 2):
                        pe.wait_ge(ps_read, S - 1)
                    tile(G_QKV + 4 * s + j, (G_QKV + j) % 2, psg[:, (1 + par) % 2], h_hi, h_lo,
                         range(4 * j, 4 * j + 4), j == 0, j == 3)
                    lags(s, par, j, lag1, lag2)

            def lags(s, par, j, lag1, lag2):
                if j == 0 and lag1:
                    pe.wait_ge(ps_read, S_QKV + s)
                    if not isinstance(s, int) or s >= 2:
                        pe.wait_ge(conv_done, s - 1)
                    for b in range(4):
                        for t in range(TT):
                            i = tr(pst[:, b, t * P:(t + 1) * P], ev[:, 1 - par, t, b * P:(b + 1) * P])
                    i.then_inc(tr_done, 1)
                if j == 1 and lag2 == "n":
                    pe.wait_ge(l2sq_done, s - 1)
                    if not isinstance(s, int) or s >= 3:
                        pe.wait_ge(ln_done, s - 2)
                    for b in range(2):
                        i = mm(psn[:, 2 * b:2 * b + 2, :], ones[:, :], sq[:, 2 * b:2 * b + 2, :], start=True, stop=True)
                    i.then_inc(nrm_done, 1)
                if j == 1 and lag2 == "v":
                    pe.wait_ge(silu_done, s - 1)
                    pe.wait_ge(ln_done, 8)
                    if not isinstance(s, int) or s > 10:
                        pe.wait_ge(vb_ev, s - 10)
                    vps = psn[:, :, :].rearrange("p (t a) b -> p t (a b)", t=TT)
                    for b in range(4):
                        for t in range(TT):
                            i = tr(vps[:, t, b * P:(b + 1) * P], sv[:, b, t * P:(t + 1) * P])
                    i.then_inc(vb_done, 1)

            qkv_slice(0, 0, False, None)
            qkv_slice(1, 1, True, None)
            with pe.Fori(0, 4) as i:
                for s in range(2):
                    qkv_slice(2 + 2 * i + s, s, True, "n")
            with pe.Fori(0, 3) as i:
                for s in range(2):
                    qkv_slice(10 + 2 * i + s, s, True, "v")

            def z_slice(z, par, lag1=False, lag2=None, kk=False):
                S = S_Z + z
                pe.wait_ge(ps_read, S - 1)
                for j in range(4):
                    tile(G_Z + 4 * z + j, (G_Z + j) % 2, psg[:, (1 + par) % 2], h_hi, h_lo,
                         range(4 * j, 4 * j + 4), j == 0, j == 3)
                    lags(NQKV + z, par, j, lag1, lag2)
                    if j == 1 and kk:
                        pe.wait_ge(kst_land, 16 * (z - 3))
                        pe.wait_ge(conv_done, NQKV)
                        pe.wait_ge(kk_ev, 4 * (z - 4))
                        for b in range(4):
                            for t in range(TT):
                                k = kst[:, b, t * P:(t + 1) * P]
                                i = mm(pst[:, b, t * P:(t + 1) * P], k, k, start=True, stop=True)
                        i.then_inc(kk_done, 1)

            z_slice(0, 0, True, "v")
            z_slice(1, 1, False, "v")
            pe.wait_ge(vb_ev, 8)
            fin(48, aacc[:, 0, :])
            z_slice(2, 0)
            z_slice(3, 1)
            with pe.Fori(2, 4) as i:
                for s in range(2):
                    z_slice(2 * i + s, s, kk=True)
            pe.wait_ge(mod_ok, 3)
            fin(64, aacc[:, 1, :])
            pe.wait_ge(mod_ok, 4)
            fin(80, aacc[:, 0, :])

            pe.wait_ge(mod_ok, 5)
            pe.wait_ge(ps_read, S_GO)
            pe.wait_ge(kk_ev, 16)
            pe.wait_ge(c_init, C_POOL)
            pe.wait_ge(c_v, C_G)
            incl = psg[:, 0, 0, 0:P].rearrange("p (t c) -> p t c", t=TT)
            cross = psg[:, 0, 0, P:2 * P].rearrange("p (t c) -> p t c", t=TT)
            for d in range(2):
                g = bt[:, 2, :, 64 + 32 * d:96 + 32 * d]
                mm(incl[:, :, 32 * d:32 * d + 32], tri[:, 2 * d, :], g, start=True, stop=True)
                i = mm(cross[:, :, 32 * d:32 * d + 32], tri[:, 2 * d + 1, :], g, start=True, stop=True)
            i.then_inc(c_p, 1)
            pe.wait_ge(c_v, C_ROWT)
            for t in range(TT):
                i = tr(psg[:, 0, 1, t * P:(t + 1) * P], rowsT[:, t, :])
            i.then_inc(c_p, 1)
            pe.wait_ge(c_v, C_ROWS)


            def step(h, par, M=True, A=True, B=True, C=True):
                b, q = h - 1, 1 - par

                def y_stage(o):
                    for c in range(4):
                        t = o if c < 2 else 1 - o
                        i = mm(ps_a[:, c, :], t64[:, q, c, t, :], rv[:, q, o, c, :], start=True, stop=True)
                    i.then_inc(y_done, 1)

                def h_stage(o):
                    pe.wait_ge(yc_done, 4 * b + 2 * o + 2)
                    for c in range(4):
                        t = o if c < 2 else 1 - o
                        i = mm(ps_b[:, c, :], dec[:, q, c, 0, 2 * t, :], yh[:, c, :], start=True, stop=True)
                    i.then_inc(h_done, 1)

                def u_stage(o):
                    pe.wait_ge(s_done, 4 * b + 2 * o + 2)
                    for c in range(4):
                        t = o if c < 2 else 1 - o
                        i = mm(ps_a[:, c, :], t64[:, q, c, t, :], rv[:, q, o, c, :], start=True, stop=True)
                    i.then_inc(u_done, 1)

                def kq(jt):
                    i = mm(psg[:, 0, jt, :], qk[:, 0, jt * P:(jt + 1) * P],
                           qk[:, :, :].rearrange("p k t -> p (k t)"), start=True, stop=True)
                    if jt:
                        i.then_inc(kq_done, 1)

                def w_stage(d):
                    pe.wait_ge(lm_done, 2 * h + d + 1)
                    for c in (2 * d, 2 * d + 1):
                        for t in range(TT):
                            i = mm(ps_w[:, 2 * c + t, :], lm[:, c, t, :], inv[:, 0, c, t, :], start=True, stop=True)
                    i.then_inc(w_done, 1)

                def t_stage(d):
                    pe.wait_ge(wt_done, 2 * h + d + 1)
                    for c in (2 * d, 2 * d + 1):
                        for t in range(TT):
                            i = mm(ps_w[:, 2 * c + t, :], wt[:, c, t, :], inv[:, 1, c, t, :], start=True, stop=True)
                    i.then_inc(t_done, 1)

                if B:
                    pe.wait_ge(rv_done, 4 * (b + 1))
                    pe.wait_ge(t64_done, b + 1)
                    y_stage(0)
                if M:
                    pe.wait_ge(qk_land, 32 * (h + 2))
                    pe.wait_ge(mk_done, h + 1)
                    kq(0)
                if B:
                    h_stage(0)
                if M:
                    kq(1)
                if B:
                    u_stage(0)
                if A:
                    pe.wait_ge(inv_land, 128 * (h + 1))
                    w_stage(0)
                if B:
                    pe.wait_ge(uc_done, 2 * b + 1)
                    for c in range(4):
                        i = mm(ps_b[:, c, :], dec[:, q, c, 0, 1, :], uu[:, 0, c, :], start=True, stop=True)
                    i.then_inc(x_done, 1)
                if A:
                    w_stage(1)
                if B:
                    pe.wait_ge(r2_done, 2 * (b + 1))
                    y_stage(1)
                if A:
                    t_stage(0)
                if B:
                    h_stage(1)
                if A:
                    t_stage(1)
                if B:
                    u_stage(1)
                    pe.wait_ge(uc_done, 2 * b + 2)
                    pe.wait_ge(aq_done, b + 1)
                    pe.wait_ge(on_done, b)
                    for t in range(TT):
                        for v in range(2):
                            terms = []
                            for d in range(2):
                                for o in range(2):
                                    tj = o if d == 0 else 1 - o
                                    if tj == t:
                                        terms.append((2 * t, 2 * d + v, o))
                                    elif o == 0:
                                        terms.append((1, 2 * d + v, o))
                            for n, (seg, c, o) in enumerate(terms):
                                i = mm(ps_o[:, 2 * t + v, :], dec[:, q, c, 1, seg, :], uu[:, o, c, :],
                                       start=n == 0, stop=n == len(terms) - 1)
                    i.then_inc(o_done, 1)
                if C:
                    pe.wait_ge(og_done, h - 1)
                    pe.wait_ge(oT_done, h - 2)
                    for v in range(2):
                        for t in range(TT):
                            i = tr(ps_oT[:, v, t * P:(t + 1) * P], og[:, 2 * t + v, :])
                    i.then_inc(ot_done, 1)
            step(-1, 1, A=False, B=False, C=False)
            step(0, 0, B=False, C=False)
            step(1, 1, C=False)
            with pe.Fori(1, HQ // 2 - 1) as i:
                for s in range(2):
                    step(2 * i + s, s)
            step(HQ - 2, 0)
            step(HQ - 1, 1, M=False)
            step(HQ, 0, M=False, A=False)
            step(HQ + 1, 1, M=False, A=False, B=False)
            pe.wait_ge(oT_done, HQ)

            with pe.Fori(0, 2) as i:
                for s in range(2):
                    n = 2 * i + s
                    pe.wait_ge(ps_read, S_GO + n - 1)
                    for j in range(8):
                        tile(G_GO + 8 * n + j, (G_GO + j) % 2, psg[:, (S_GO + s) % 2], o_hi, o_lo,
                             range(4 * j, 4 * j + 4), j == 0, j == 7, ready=(osp_lo, j + 1))

            def ffn(f, g0, s0, n_pre):
                def sl(S, par, g, kcs_tiles, a_hi, a_lo, ready=None, after=None):
                    pe.wait_ge(ps_read, S - 1)
                    for j, kcs in enumerate(kcs_tiles):
                        tile(g + j, (g0 + par[1] + j) % 2, psg[:, (s0 + par[0]) % 2], a_hi, a_lo, kcs, j == 0,
                             j == len(kcs_tiles) - 1, ready=ready and ready(j))
                        if after:
                            after(j)
                whole = [range(4 * j, 4 * j + 4) for j in range(4)]
                sl(s0, (0, 0), g0, whole, h_hi3, h_lo3, ready=lambda j: (pre_lo, 4 * n_pre + j + 1))
                sl(s0 + 1, (1, 4), g0 + 4, whole, h_hi3, h_lo3)

                def turn(n):
                    pe.wait_ge(ps_read, s0 + 6 * n + 2)
                    pe.wait_ge(g_lo_ok, GRP * f + n)
                    for b in range(4):
                        for t in range(TT):
                            i = tr(pst[:, b, t * P:(t + 1) * P], gg[:, t, b * P:(b + 1) * P])
                    i.then_inc(g_tr, 1)

                def outs(n, S, par, g, gpar):
                    for j in range(4):
                        sl(S + j, (par + j, gpar + j), g + j, [range(4)], g_hi, g_lo,
                           ready=lambda _: (g_lo_ok, GRP * f + n + 1))

                with pe.Fori(0, (GRP - 1) // 2) as i:
                    for s in range(2):
                        n = 2 * i + s + 1
                        S, g = s0 + 2 + 12 * i + 6 * s, g0 + 8 + 24 * i + 12 * s
                        sl(S, (0, 0), g, whole, h_hi3, h_lo3, after=lambda j: turn(n - 1) if j == 0 else None)
                        outs(n - 1, S + 1, 1, g + 4, 0)

                        def last(j):
                            if f == 0 and s == 1 and j == 2:
                                pe.wait_ge(mod_ok, 5 + i)
                                fin(102 + 18 * i, aacc3[:, 1, :])
                        sl(S + 5, (1, 0), g + 8, whole, h_hi3, h_lo3, after=last)
                turn(GRP - 1)
                pe.wait_ge(mod_ok, 10 + f)
                fin(176 + 16 * f, aacc3[:, 0, :])
                outs(GRP - 1, s0 + 2 + 6 * (GRP - 1), 0, g0 + 8 + 12 * (GRP - 1), 0)

            pre(1, y)
            ffn(0, G_F0, S_F0, 1)
            pre(2, y)
            def turn2(ready, src, dst, done, free):
                pe.wait_ge(*ready)
                if free:
                    pe.wait_ge(*free)
                for b in range(4):
                    for t in range(TT):
                        i = tr(dst[:, b, t * P:(t + 1) * P], src[:, t, b * P:(b + 1) * P])
                i.then_inc(done, 1)

            def pw1_pair(n, lag):
                for j in range(8):
                    if j % 4 == 0:
                        pe.wait_ge(ps_read, S_P1 + 2 * n + j // 4 - 1)
                    tile(G_P1 + 8 * n + j, (G_P1 + j) % 2, psg[:, (S_P1 + j // 4) % 2], h_hi3, h_lo3,
                         range(4 * (j % 4), 4 * (j % 4) + 4), j % 4 == 0, j % 4 == 3,
                         ready=(pre_lo, 8 + j % 4 + 1))
                    if j == 0 and lag:
                        turn2((ps_read, S_P1 + 2 * n), ev4[:, 1], psn, t_g, (sg_ok, n - 1))
                    if j == 4:
                        turn2((ps_read, S_P1 + 2 * n + 1), ev4[:, 0], pst, t_a, (glu_ok, n))
            pw1_pair(0, False)
            with pe.Fori(1, 4) as i:
                pw1_pair(i, True)
            turn2((ps_read, S_P2), ev4[:, 1], psn, t_g, (sg_ok, 3))
            pe.wait_ge(sg_ok, 4)
            pe.wait_ge(glu_ok, 4)
            for kc in range(KC):
                if kc % 4 == 0 and kc >= 8:
                    pe.wait_ge(dw_ok, kc // 4 + 1)
                i = mm(pst[:, 0, :], ones[:, :], dwo[:, kc, :], start=kc == 0, stop=kc == KC - 1)
            i.then_inc(ln_p, 1)
            for q in range(4):
                pe.wait_ge(ln_s, q + 1)
                for j in range(4):
                    i = mm(pst[:, 2, :], ones[:, :], hf3[:, q % 2, j, :], start=q + j == 0, stop=q + j == 6)
                i.then_inc(ln_p, 1)
            with pe.Fori(0, 2) as i:
                for s in range(2):
                    n = 2 * i + s
                    pe.wait_ge(ps_read, S_P2 + n - 1)
                    for j in range(4):
                        tile(G_P2 + 4 * n + j, (G_P2 + j) % 2, psg[:, (S_P2 + s) % 2], h_hi3, h_lo3,
                             range(4 * j, 4 * j + 4), j == 0, j == 3, ready=(pre_lo, 12 + j + 1))
            pre(3, y)
            ffn(1, G_F1, S_F1, 4)

        @block.vector
        def _(dve):
            tt, ts, stt = nc.vector.tensor_tensor, nc.vector.tensor_scalar, nc.vector.scalar_tensor_tensor

            def lo(g, j):
                dve.wait_ge(w_hi, g + 1)
                tt(wlo[:, j % 2, :], wraw[:, j % 4, :], whi[:, j % 2, :].bitcast(F32), SUB).then_inc(w_lo, 1)

            def ada(a, par, ring, acc, k, first=False):
                dve.wait_ge(a_land[par], 8 * (a - 2 * KC - par) + 16)
                c = cond[:, ds(k, 1)]
                if first:
                    ts(acc, ring[:, par, :], c, None, MUL).then_inc(a_used, 1)
                else:
                    dve.wait_ge(a_used, a)
                    stt(acc, ring[:, par, :], c, acc, MUL, ADD).then_inc(a_used, 1)

            def mod_add(n, flat):
                dve.wait_ge(a_fin, n)
                tt(mod[:, ds(flat, 1), :].rearrange("p a k -> p (a k)"), psn[:, 0, 0:KC],
                   vec[:, ds(NV_ADAB + flat * KC, KC)], ADD).then_inc(mod_ok, 1)

            def pre(n, xn, hi, lo_, hfb, mods, low0, weights=None):
                dve.wait_ge(mod_ok, mods)
                stt(aff[:, n, :], mod[:, 3 * n + 1, :], 1.0, vec[:, NV_NORM + 2 * n * KC:NV_NORM + (2 * n + 1) * KC],
                    ADD, MUL).then_inc(aff_ok, 1)
                for t in range(TT):
                    dve.wait_ge(sq_ok, TT * n + t + 1)
                    r = st[:, 2 * n, t:t + 1]
                    ts(r, r, 1.0 / D, RMS_EPS, MUL, ADD).then_inc(ms_ok, 1)
                    dve.wait_ge(rt_ok, TT * n + t + 1)
                    nc.vector.reciprocal(r, r).then_inc(rs_ok, 1)
                    dve.wait_ge(rs_ok, TT * n + t + 1)
                    ts(xn[:, t, :], x[:, t, :], r, None, MUL).then_inc(xn_ok, 1)
                dve.wait_ge(aff_ok, n + 1)

                def low(q):
                    dve.wait_ge((hf_v, hf_s)[q % 2], 2 * n + q // 2 + 1)
                    dve.wait_ge(pre_hi, 4 * n + q + 1)
                    tt(lo_[:, 4 * q:4 * q + 4, :], hfb[:, q % 2], hi[:, 4 * q:4 * q + 4, :].bitcast(F32),
                       SUB).then_inc(pre_lo, 1)
                for q in (0, 2):
                    dve.wait_ge(pre_tr, 4 * n + q + 1)
                    if q:
                        dve.wait_ge(pre_lo, low0 + 1)
                    for j in range(4):
                        kc = 4 * q + j
                        i = ts(hfb[:, 0, j, :], pst[:, j, :], aff[:, n, kc:kc + 1], mod[:, 3 * n, kc:kc + 1], MUL, ADD)
                    i.then_inc(hf_v, 1)
                    if q == 0 and weights:
                        weights()
                    low(q // 2)
                low(2)
                low(3)

            def post_col(n, j, yb, cw):
                dve.wait_ge(yq_ok, 8 * n + 2 * j + 2)
                yj = yb[:, :, j * NSL:(j + 1) * NSL]
                tt(yj, yj, cw[:, j * NSL:(j + 1) * NSL].unsqueeze(1).broadcast_to([P, TT, NSL]), MUL).then_inc(yc_ok, 1)

            def post(n, yb, cw):
                r = st[:, 2 * n + 1, :]
                dve.wait_ge(yq_ok, 8 * (n + 1))
                nc.vector.tensor_reduce(r, spart[:, :, :], axis=AX, op=ADD).then_inc(yr_ok, 1)
                dve.wait_ge(yr_ok, 3 * n + 1)
                ts(r, r, 1.0 / D, RMS_EPS, MUL, ADD).then_inc(yr_ok, 1)
                post_col(n, 3, yb, cw)
                dve.wait_ge(yrt_ok, n + 1)
                nc.vector.reciprocal(r, r).then_inc(yr_ok, 1)
                dve.wait_ge(yr_ok, 3 * n + 3)
                dve.wait_ge(yc_ok, 4 * (n + 1))
                for t in range(TT):
                    stt(x[:, t, :], yb[:, t, :], st[:, 2 * n + 1, t:t + 1], x[:, t, :], MUL, ADD).then_inc(x_up, 1)

            def cw_col(n, mods):
                dve.wait_ge(mod_ok, mods)
                stt(cwc[:, n, :], mod[:, 3 * n + 2, :], 1.0,
                    vec[:, NV_NORM + (2 * n + 1) * KC:NV_NORM + (2 * n + 2) * KC], ADD, MUL).then_inc(cwc_ok, 1)

            dve.wait_ge(vec_tr, 1)
            vps = psg[:, :, :, :].rearrange("p a b n -> p (a b n)")
            for n, (at, w) in enumerate(((0, 128), (128, 96), (224, 96), (320, 16), (336, 128), (464, 128), (592, 64),
                                         (656, 128), (784, 128), (912, 128), (1040, 112), (1152, 80))):
                i = nc.vector.tensor_copy(vec[:, at:at + w], vps[:, n * P:n * P + w])
            i.then_inc(vec_ok, 1)
            for n in range(2):
                nc.vector.memset(aacc[:, n, :], 0.0).then_inc(a_zero, 1)
            dve.wait_ge(cond_ok, 1)
            dve.wait_ge(a_zero, 2)
            for n in range(2):
                for k in range(KC):
                    a = KC * n + k
                    dve.wait_ge(a0_land[a % 4], 16 * (a // 4 + 1))
                    if k:
                        dve.wait_ge(a_used, a)
                    stt(aacc[:, n, :], aring0[:, a % 4, :], cond[:, k:k + 1], aacc[:, n, :], MUL, ADD).then_inc(a_used, 1)
            mod_add(1, 0)
            mod_add(2, 1)
            pre(0, y1, h_hi, h_lo, hf, 2, 0)
            nc.vector.memset(aacc[:, 0, :], 0.0).then_inc(a_zero, 1)
            lo(0, 0)
            lo(1, 1)
            dve.wait_ge(w_used, 1)
            nc.vector.tensor_copy(ba[:, :, :], psg[:, 0, :, 0:P]).then_inc(ps_read, 1)
            dve.wait_ge(a_zero, 3)

            taps = Tally(tap)

            def conv(s, par, blocks):
                if blocks[0] == 0:
                    dve.wait_ge(tr_done, s + 1)
                    if not isinstance(s, int) or s >= 2:
                        dve.wait_ge(silu_done, s - 1)
                for n, k in enumerate((2, 0, 1, 3, 4)):
                    off = k - 2
                    a, b = max(0, -off), T - max(0, off)
                    if n:
                        dve.wait_ge(tap, taps.at())
                    for blk in blocks:
                        w = vec[:, ds(NV_CONV + k * (QKV // P) + 4 * s + blk, 1)]
                        src, dst = pst[:, blk, a + off:b + off], cv[:, par, blk, a:b]
                        if n == 0:
                            i = ts(dst, src, w, None, MUL)
                        else:
                            i = stt(dst, src, w, dst, MUL, ADD)
                        if n == 4 and blk == 3:
                            i.then_inc(conv_done, 1)
                        else:
                            taps.inc(i)

            def qkv_slice(s, par, lag):
                g = G_QKV + 4 * s
                if not (isinstance(s, int) and s == 0):
                    lo(g, G_QKV)
                ada(32 + s, par, aring, aacc[:, 0, :], s)
                lo(g + 1, G_QKV + 1)
                if lag:
                    conv(s - 1, 1 - par, (0,))
                lo(g + 2, G_QKV + 2)
                if lag:
                    conv(s - 1, 1 - par, (1, 2))
                lo(g + 3, G_QKV + 3)
                if lag:
                    conv(s - 1, 1 - par, (3,))

            qkv_slice(0, 0, False)
            qkv_slice(1, 1, True)
            with taps.loop(dve, 0, 7, 2 * 19) as i:
                for s in range(2):
                    qkv_slice(2 + 2 * i + s, s, True)

            def z_slice(z, par, n, lag=False, extra=None):
                for j in range(4):
                    lo(G_Z + 4 * z + j, G_Z + j)
                    if lag and j >= 2:
                        conv(NQKV - 1, 1, (2 * j - 4, 2 * j - 3))
                    if extra and j == 0:
                        extra()
                    ada(48 + 4 * z + j, j % 2, aring, aacc[:, n, :], (4 * z + j) if isinstance(z, int) else z * 4 + j - 16)

            nc.vector.memset(aacc[:, 1, :], 0.0).then_inc(a_zero, 1)
            dve.wait_ge(a_zero, 4)
            z_slice(0, 0, 1, lag=True)
            z_slice(1, 1, 1)
            z_slice(2, 0, 1, extra=lambda: mod_add(3, 2))
            z_slice(3, 1, 1)
            nc.vector.memset(aacc[:, 0, :], 0.0).then_inc(a_zero, 1)
            dve.wait_ge(a_zero, 5)
            with dve.Fori(2, 4) as i:
                for s in range(2):
                    z_slice(2 * i + s, s, 0)
            mod_add(4, 3)
            mod_add(5, 4)
            cw_col(0, 5)

            pr = Tally(c_v)

            def dvh(ap):
                return ap.rearrange("p (d h v) -> p d v h", d=2, v=2)

            def dv(ap):
                return ap.rearrange("p (d v) h -> p d v h", d=2)
            dve.wait_ge(c_land, 64)
            pr.inc(nc.vector.tensor_copy(bt[:, 0, :, 0:64], ba2[:, :, 0:64]))
            pr.inc(tt(bt[:, 0, :, 64:128], ba2[:, :, 64:128], alog[:, 1:2, :].broadcast_to([P, TT, 64]), ADD))
            pr.wait(dve)
            pr.inc(ts(bt[:, 0, :, 64:128], bt[:, 0, :, 64:128], -1.0, None, MUL))
            dve.wait_ge(c_s, 4)
            pr.wait(dve)
            flat = "p a b -> p (a b)"
            pr.inc(stt(bt[:, 2].rearrange(flat), bt[:, 0].rearrange(flat), 0.0, bt[:, 1].rearrange(flat), MIN, SUB))
            pr.wait(dve)
            pr.inc(tt(bt[:, 2, :, 64:128], bt[:, 2, :, 64:128], alog[:, 0:1, :].broadcast_to([P, TT, 64]), MUL))
            assert pr.n == C_G
            incl = psg[:, 0, 0, 0:P].rearrange("p (t c) -> p t c", t=TT)
            cross = psg[:, 0, 0, P:2 * P].rearrange("p (t c) -> p t c", t=TT)
            dve.wait_ge(c_p, 1)
            dve.wait_ge(c_init, C_POOL)
            for t in range(TT):
                pr.inc(ts(dv(ncum[:, 0, t]), dvh(incl[:, t]), -1.0, None, MUL))
                pr.inc(nc.vector.tensor_copy(dv(ncum[:, 1, t]), dvh(cross[:, t])))
            for t in range(TT):
                r = rowsT[:, t, :].rearrange("p (d v k h) -> p d v k h", d=2, v=2, k=2)
                pr.inc(tt(r[:, :, :, 0, :], dvh(incl[:, t]), dvh(bt[:, 2, t, 0:64]), ADD))
                pr.inc(nc.vector.tensor_copy(r[:, :, :, 1, :], dvh(incl[:, t])))
            assert pr.n == C_ROWT
            dve.wait_ge(c_p, 2)
            pr.inc(nc.vector.tensor_copy(rows[:, :], psg[:, 0, 1, 0:T]))
            assert pr.n == C_ROWS
            dve.wait_ge(s_land, 16)
            sr4 = srow[:, :, :].rearrange("p (c k) i -> p c k i", k=2)
            for d in range(2):
                pr.inc(tt(sdec[:, 2 * d:2 * d + 2],
                          sr4[:, 2 * d:2 * d + 2, 0, :].unsqueeze(3).broadcast_to([P, 2, 32, 32]),
                          sr4[:, 2 * d:2 * d + 2, 1, :].unsqueeze(2).broadcast_to([P, 2, 32, 32]), SUB))
            pr.wait(dve)
            sflat = sdec[:, :, :, :].rearrange("p c i j -> p (c i j)")
            pr.inc(ts(sflat, sflat, 0.0, None, MIN))
            assert pr.n == C_SUB
            dve.wait_ge(c_s, 7)
            for c in range(4):
                s1 = sdec[:, c].rearrange("p i j -> p (i j)")
                pr.inc(stt(s1, skk[:, :, :].rearrange("p i j -> p (i j)"), -1.0, s1, MUL, MUL))
            assert pr.n == C_DEC
            invert(dve, nc.vector, pr, ((0, 0, 2), (1, 0, 1)))
            assert pr.n == C_INV

            mkf = mk[:, :, :, :, :].rearrange("p d k s m -> p d k (s m)")
            mmf = masks[:, :, :, :, :].rearrange("p d k s m -> p d k (s m)")
            kqf = psg[:, 0, :, :].rearrange("p t (k n) -> p t k n", k=2)

            def step(h, par, M=True, A=True, B=True, C=True):
                b, p = h - 1, 1 - par

                def second_half(o):
                    dve.wait_ge(h_done, 2 * b + o + 1)
                    for d in range(2):
                        q = slice(64, P) if d == 0 else slice(0, 64)
                        tt(rv[q, p, o, 2 * d:2 * d + 2, :], ps_b[q, 2 * d:2 * d + 2, :], rv[q, p, o, 2 * d:2 * d + 2, :],
                           ADD).then_inc(s_done, 1)

                def mask(d):
                    tt(mkf[:, d, :, d * P:(d + 2) * P], kqf[:, d], mmf[:, d, :, d * P:(d + 2) * P], MUL)
                    n = 2 - 2 * d
                    return tt(mkf[:, d, :, n * P:(n + 1) * P], kqf[:, 1 - d, :, (1 - d) * P:(2 - d) * P],
                              mmf[:, d, :, n * P:(n + 1) * P], MUL)

                if A:
                    dve.wait_ge(d0_done, h + 1)
                    dve.wait_ge(mk_done, h + 1)
                    for c in range(4):
                        f = dec[:, par, c, 0].rearrange("p s m -> p (s m)")
                        i = tt(f, f, mk[:, c // 2, 0].rearrange("p s m -> p (s m)"), MUL)
                    i.then_inc(la_done, 1)
                if B:
                    dve.wait_ge(rv_done, 4 * (b + 1))
                    second_half(0)
                if A:
                    dve.wait_ge(la_done, h + 1)
                    dve.wait_ge(w_done, 2 * h)
                    for d in range(2):
                        for v in range(2):
                            i = tt(lm[:, 2 * d + v, :, :], dec[:, par, 2 * d + v, 0, 0:3:2, :],
                                   m64[:, d:d + 1, :].broadcast_to([P, TT, P]), MUL)
                        i.then_inc(lm_done, 1)
                if M:
                    dve.wait_ge(kq_done, h + 2)
                    dve.wait_ge(aq_done, h + 1)
                    mask(0)
                if B:
                    dve.wait_ge(x_done, b + 1)
                    for d in range(2):
                        tt(rv[:, p, 1, 2 * d:2 * d + 2, :], ps_b[:, 2 * d:2 * d + 2, :], rv[:, p, 1, 2 * d:2 * d + 2, :],
                           ADD).then_inc(r2_done, 1)
                if M:
                    mask(1).then_inc(mk_done, 1)
                if C:
                    dve.wait_ge(osq_done, h - 1)
                    nc.vector.tensor_reduce(oms[:, 0, :], osq[:, :, :], axis=AX, op=ADD).then_inc(oms_done, 1)
                if B:
                    second_half(1)
                if A:
                    dve.wait_ge(t_done, 2 * h + 2)
                    tt(t64[:, par].rearrange("p c t m -> p (c t) m"), ps_w,
                       inv[:, 1].rearrange("p c t m -> p (c t) m"), ADD).then_inc(t64_done, 1)
                if C:
                    dve.wait_ge(ors_done, h - 1)
                    dve.wait_ge(ot_done, h - 2)
                    tt(og[:, :, :], ps_o, oms[:, 2, :].unsqueeze(2).broadcast_to([P, 4, P]), MUL).then_inc(on_done, 1)
                if M:
                    dve.wait_ge(rr_land, 16 * (h + 2))
                    dve.wait_ge(d1_done, h + 1)
                    for c in range(4):
                        for seg, t, kind, tj in ((0, 0, 0, 0), (2, 1, 0, 1), (1, 1 - c // 2, 1, c // 2)):
                            i = ts(exb[:, c, :, seg, :], rr[:, 2 * c:2 * c + 2, t * P:(t + 1) * P],
                                   ncum[:, kind, tj, c, ds(h + 1, 1)], 0.0, ADD, MIN)
                    i.then_inc(ex_done, 1)
            step(-1, 1, A=False, B=False, C=False)
            step(0, 0, B=False, C=False)
            step(1, 1, C=False)
            with dve.Fori(1, HQ // 2 - 1) as i:
                for s in range(2):
                    step(2 * i + s, s)
            step(HQ - 2, 0)
            step(HQ - 1, 1, M=False)
            step(HQ, 0, M=False, A=False)
            step(HQ + 1, 1, M=False, A=False, B=False)

            dve.wait_ge(oT_done, HQ)
            lo(G_GO, G_GO)
            lo(G_GO + 1, G_GO + 1)
            for q in range(8):
                dve.wait_ge(osp_hi, q + 1)
                tt(o_lo[:, 4 * q:4 * q + 4, :], oT[:, 4 * q:4 * q + 4, :], o_hi[:, 4 * q:4 * q + 4, :].bitcast(F32),
                   SUB).then_inc(osp_lo, 1)
            for j in range(2, 8):
                lo(G_GO + j, G_GO + j)
            dve.wait_ge(cw_land, 16)
            for n in range(1, 4):
                for j in range(8):
                    lo(G_GO + 8 * n + j, G_GO + j)
                    if j == 6:
                        post_col(0, n - 1, yg, cwb0)
            lo(G_F0, G_F0)
            post(0, yg, cwb0)
            pre(1, y, h_hi3, h_lo3, hf3, 5, 4, lambda: lo(G_F0 + 1, G_F0 + 1))

            def ffn(f, g0, s0):
                nm = GRP * f
                nc.vector.memset(y[:, :, :], 0.0).then_inc(y_zero, 1)
                dve.wait_ge(y_zero, f + 1)

                def mul(n, S, g_end):
                    dve.wait_ge(w_used, g_end)
                    dve.wait_ge(ps_read, S)
                    if f or not isinstance(n, int):
                        dve.wait_ge(g_tr, nm + n)
                    tt(gg[:, :, :], psg[:, (s0 + 1) % 2], sg[:, :, :], MUL).then_inc(ps_read, 1)

                def g_low(n):
                    dve.wait_ge(g_hi_ok, nm + n + 1)
                    tt(g_lo[:, :, :], pst[:, :, :], g_hi[:, :, :].bitcast(F32), SUB).then_inc(g_lo_ok, 1)

                def y_sum(S, g_end, par, j, n):
                    dve.wait_ge(w_used, g_end)
                    yj = y[:, :, j * NSL:(j + 1) * NSL]
                    dve.wait_ge(ps_read, S)
                    tt(yj, psg[:, (s0 + par) % 2], yj, ADD).then_inc(ps_read, 1)

                for j in range(8):
                    if j >= 2:
                        lo(g0 + j, g0 + j)
                    if j < 6:
                        ada((80, 176)[f] + j, j % 2, aring3, aacc3[:, 0, :], j, first=j == 0)
                with dve.Fori(0, (GRP - 1) // 2) as i:
                    at = 0
                    for s in range(2):
                        n = 2 * i + s + 1
                        S, g = s0 + 2 + 12 * i + 6 * s, g0 + 8 + 24 * i + 12 * s
                        for j in range(12):
                            if 6 <= j < 10:
                                y_sum(S + j - 5, g + j - 1, j - 5, j - 6, n - 1)
                            lo(g + j, g0 + j)
                            if j == 0:
                                mul(n - 1, S - 1, g)
                            if j == 2:
                                g_low(n - 1)
                            if f and j == 6:
                                ada(182 + 2 * i + s, s, aring3, aacc3[:, 0, :], 6 + 2 * i + s)
                            if f == 0 and j in ADA_AT:
                                if at < 16:
                                    ada(86 + 18 * i + at, at % 2, aring3, aacc3[:, 1, :], at, first=at == 0)
                                else:
                                    ada(86 + 18 * i + at, at % 2, aring3, aacc3[:, 0, :], 6 + 2 * i + at - 16)
                                at += 1
                    if f == 0:
                        mod_add(6 + i, 6 + i)
                gl, Sl = g0 + 8 + 12 * (GRP - 1), s0 + 2 + 6 * (GRP - 1)
                lo(gl, g0)
                mul(GRP - 1, Sl - 1, gl)
                lo(gl + 1, g0 + 1)
                g_low(GRP - 1)
                mod_add(11 + f, 5 + 6 * f)
                cw_col(1 + 2 * f, 11 + f)
                for j in range(4):
                    y_sum(Sl + j, gl + j + 1, j, j, GRP - 1)
                    if j < 2:
                        lo(gl + j + 2, g0 + j + 2)
                    if j == 2:
                        if f == 0:
                            lo(G_P1, G_P1)
                        dve.wait_ge(cw_land, 16 * (2 * f + 2))
                        post_col(2 * f + 1, 0, y, cwb)
                post_col(2 * f + 1, 1, y, cwb)
                post_col(2 * f + 1, 2, y, cwb)

            ffn(0, G_F0, S_F0)
            post(1, y, cwb)
            pre(2, y, h_hi3, h_lo3, hf3, 11, 8, lambda: lo(G_P1 + 1, G_P1 + 1))
            cw_col(2, 11)
            dwt = Tally(tap, taps.n)

            def unit(n):
                dve.wait_ge(sg_ok, n + 1)
                dve.wait_ge(t_a, n + 1)
                dve.wait_ge(dw_ok, n)
                dve.wait_ge(dwp_ok, len(TAPS_S) * n)
                for b in range(4):
                    i = stt(glu[:, b, :], pst[:, b, :], vec[:, ds(V_PW1B + 4 * n + b, 1)], sg4[:, b, :], ADD, MUL)
                i.then_inc(glu_ok, 1)
                dve.wait_ge(glu_ok, n + 1)

            order = list(enumerate(TAPS_V))

            def dw(n, part):
                for m, k in part:
                    off = k - CTAPS // 2
                    a, e = max(0, -off), T - max(0, off)
                    if m:
                        dve.wait_ge(tap, dwt.at())
                    for b in range(4):
                        w = vec[:, ds(NV_DW + k * KC + 4 * n + b, 1)]
                        src = glu[:, b, a + off:e + off]
                        dst = dwo[:, ds(4 * n + b, 1), a:e].rearrange("p a t -> p (a t)")
                        if m == 0:
                            i = ts(dst, src, w, vec[:, ds(V_DWB + 4 * n + b, 1)], MUL, ADD)
                        else:
                            i = stt(dst, src, w, dst, MUL, ADD)
                    dwt.inc(i)
                if part and part[-1][0] == len(TAPS_V) - 1:
                    dve.wait_ge(tap, dwt.at())
                    dve.wait_ge(dwa_ok, (len(TAPS_S) + 1) * (n + 1))
                    dst = dwo[:, ds(4 * n, 4), :]
                    tt(dst, dst, dwa, ADD).then_inc(dw_ok, 1)

            def pw1_pair(n, lag):
                for j in range(8):
                    if lag or j >= 2:
                        lo(G_P1 + 8 * n + j, G_P1 + j)
                    if lag and j == 1:
                        unit(n - 1)
                    if lag and j >= 1:
                        dw(n - 1, order[(j - 1) * 3:j * 3])
            pw1_pair(0, False)
            with dwt.loop(dve, 1, 4, len(TAPS_V)) as i:
                pw1_pair(i, True)
            unit(3)
            dw(3, order)
            lv = Tally(ln_v)
            dve.wait_ge(ln_p, 1)
            lv.inc(ts(lnst[:, 0, :], pst[:, 0, :], 1.0 / D, None, MUL))
            lv.wait(dve)
            dve.wait_ge(dw_ok, 4)
            for q in range(4):
                d4 = dwo[:, 4 * q:4 * q + 4, :]
                lv.inc(tt(d4, d4, lnst[:, 0:1, :].broadcast_to([P, 4, T]), SUB))
            dve.wait_ge(ln_p, 5)
            lv.inc(ts(lnst[:, 1, :], pst[:, 2, :], 1.0 / D, LN_EPS, MUL, ADD))
            dve.wait_ge(ln_s, 5)
            lv.inc(nc.vector.reciprocal(lnst[:, 1, :], lnst[:, 1, :]))
            lv.wait(dve)
            for q in range(4):
                d4 = dwo[:, 4 * q:4 * q + 4, :]
                lv.inc(tt(d4, d4, lnst[:, 1:2, :].broadcast_to([P, 4, T]), MUL))
            for j in range(2):
                lo(G_P2 + j, G_P2 + j)
            for q in range(4):
                dve.wait_ge(ln_s, 5 + 2 * (q + 1))
                tt(h_lo3[:, 4 * q:4 * q + 4, :], hf3[:, q % 2], h_hi3[:, 4 * q:4 * q + 4, :].bitcast(F32),
                   SUB).then_inc(pre_lo, 1)
            dve.wait_ge(pb_land, 16)

            def y_bias(n, par):
                dve.wait_ge(w_used, G_P2 + 4 * n + 4)
                for t in range(TT):
                    i = tt(y[:, t, ds(n * NSL, NSL)], psg[:, (S_P2 + par) % 2, t, :], pw2b[:, ds(n * NSL, NSL)], ADD)
                i.then_inc(ps_read, 1)
            lo(G_P2 + 2, G_P2 + 2)
            lo(G_P2 + 3, G_P2 + 3)
            for n in range(1, 4):
                lo(G_P2 + 4 * n, G_P2)
                lo(G_P2 + 4 * n + 1, G_P2 + 1)
                y_bias(n - 1, (n - 1) % 2)
                lo(G_P2 + 4 * n + 2, G_P2 + 2)
                lo(G_P2 + 4 * n + 3, G_P2 + 3)
                if n == 1:
                    dve.wait_ge(cw_land, 48)
                post_col(2, n - 1, y, cwb)
            lo(G_F1, G_F1)
            y_bias(3, 1)
            post(2, y, cwb)
            pre(3, y, h_hi3, h_lo3, hf3, 11, 16, lambda: lo(G_F1 + 1, G_F1 + 1))
            ffn(1, G_F1, S_F1)
            post(3, y, cwb)

        @block.scalar
        def _(act):
            av = nc.scalar.activation

            def hi(g, j):
                act.wait_ge(w_land[j % 4], 4 * (g - j % 4) + 16)
                if not isinstance(g, int) or g >= 2:
                    act.wait_ge(w_used, g - 1)
                av(whi[:, j % 2, :], wraw[:, j % 4, :], ACT.Copy).then_inc(w_hi, 1)

            dump = psg[:, :, :, :].rearrange("p a b n -> p (a b n)")

            def squares(n, ready):
                for t in range(TT):
                    act.wait_ge(*ready(t))
                    if n or t:
                        act.wait_ge(sq_ok, TT * n + t)
                    av(dump, x[:, t, :], ACT.Square, accum_out=st[:, 2 * n, t:t + 1]).then_inc(sq_ok, 1)
                for t in range(TT):
                    act.wait_ge(ms_ok, TT * n + t + 1)
                    av(st[:, 2 * n, t:t + 1], st[:, 2 * n, t:t + 1], ACT.Sqrt).then_inc(rt_ok, 1)

            def out_squares(n, j, yb, dump_at, ready):
                act.wait_ge(*ready)
                for t in range(TT):
                    if 8 * n + 2 * j + t:
                        act.wait_ge(yq_ok, 8 * n + 2 * j + t)
                    if n and j + t == 0:
                        act.wait_ge(yr_ok, 3 * n)
                    av(dump_at, yb[:, t, j * NSL:(j + 1) * NSL], ACT.Square, accum_out=spart[:, t, j:j + 1]
                       ).then_inc(yq_ok, 1)

            def out_root(n):
                act.wait_ge(yr_ok, 3 * n + 2)
                av(st[:, 2 * n + 1, :], st[:, 2 * n + 1, :], ACT.Sqrt).then_inc(yrt_ok, 1)

            def pre(n, hi_, hfb, low0):
                act.wait_ge(aff_ok, n + 1)

                def odd(q):
                    act.wait_ge(pre_tr, 4 * n + q + 1)
                    if q == 3:
                        act.wait_ge(pre_lo, low0 + 2)
                    for j in range(4):
                        kc = 4 * q + j
                        i = av(hfb[:, 1, j, :], psn[:, j, :], ACT.Identity, bias=mod[:, 3 * n, kc:kc + 1],
                               scale=aff[:, n, kc:kc + 1])
                    i.then_inc(hf_s, 1)

                def high(q):
                    act.wait_ge((hf_v, hf_s)[q % 2], 2 * n + q // 2 + 1)
                    av(hi_[:, 4 * q:4 * q + 4, :], hfb[:, q % 2], ACT.Copy).then_inc(pre_hi, 1)
                odd(1)
                high(0)
                high(1)
                high(2)
                odd(3)
                high(3)

            act.wait_ge(init, 7)
            act.wait_ge(vec_ok, 1)
            av(cond[:, :], vec[:, NV_C:NV_C + KC], ACT.Silu).then_inc(cond_ok, 1)
            squares(0, lambda t: (x_land, 16))
            pre(0, h_hi, hf, 0)
            hi(0, 0)
            hi(1, 1)

            def qk_silu(s, par):
                act.wait_ge(conv_done, s + 1)
                act.wait_ge(kn_ready, s)
                av(sv[:, :, :], cv[:, par, :, :], ACT.Silu).then_inc(silu_done, 1)
                act.wait_ge(silu_done, s + 1)
                act.wait_ge(nrm_done, s)
                av(sq[:, :, :], sv[:, :, :], ACT.Square).then_inc(l2sq_done, 1)

            def v_silu(s, par):
                act.wait_ge(conv_done, s + 1)
                act.wait_ge(kn_ready, 8)
                act.wait_ge(vb_done, s - 8)
                av(sv[:, :, :], cv[:, par, :, :], ACT.Silu).then_inc(silu_done, 1)

            def qk_log(s):
                act.wait_ge(nrm_done, s + 1)
                act.wait_ge(kn_ready, s)
                av(rn[:, :, :], psn[:, :, :], ACT.Ln, bias=epsr[:, 0:1]).then_inc(ln_done, 1)

            def qk_norm(s):
                act.wait_ge(ln_done, s + 1)
                av(rn[:, :, :], rn[:, :, :], ACT.Exp, scale=-0.5).then_inc(rn_done, 1)

            def v_back(s):
                act.wait_ge(vb_done, s - 7)
                act.wait_ge(kn_out, 16 * s)
                av(kn[:, :, :], psn[:, :, :], ACT.Copy).then_inc(vb_ev, 1)

            def evac(s, par):
                act.wait_ge(w_used, G_QKV + 4 * s + 4)
                act.wait_ge(ps_read, S_QKV + s)
                if not isinstance(s, int) or s >= 2:
                    act.wait_ge(tr_done, s - 1)
                av(ev[:, par, :, :], psg[:, (1 + par) % 2, :, :], ACT.Copy).then_inc(ps_read, 1)

            def z_evac(z, par):
                act.wait_ge(w_used, G_Z + 4 * z + 4)
                act.wait_ge(ps_read, S_Z + z)
                if isinstance(z, int) and z < 2:
                    act.wait_ge(tr_done, 15 + z)
                else:
                    act.wait_ge(zw_done, z - 1)
                av(ev[:, par, :, :], psg[:, (1 + par) % 2, :, :], ACT.Silu).then_inc(ps_read, 1)

            def a_slice(g, g0, first, after0, after1, after3, after2=None):
                for j in range(4):
                    if j or not first:
                        hi(g + j, g0 + j)
                    for n, f in ((0, after0), (1, after1), (2, after2), (3, after3)):
                        if j == n and f:
                            f()

            def qkv_slice(s, par, kind):
                def a0():
                    (qk_silu if kind == "n" else v_silu)(s - 2, par)
                a_slice(G_QKV + 4 * s, G_QKV, isinstance(s, int) and s == 0, a0 if kind else None,
                        (lambda: evac(s - 1, 1 - par)) if not (isinstance(s, int) and s == 0) else None,
                        (lambda: (qk_norm if kind == "n" else v_back)(s - 2)) if kind else None,
                        (lambda: qk_log(s - 2)) if kind == "n" else None)
            qkv_slice(0, 0, None)
            qkv_slice(1, 1, None)
            with act.Fori(0, 4) as i:
                for s in range(2):
                    qkv_slice(2 + 2 * i + s, s, "n")
            with act.Fori(0, 3) as i:
                for s in range(2):
                    qkv_slice(10 + 2 * i + s, s, "v")

            a_slice(G_Z, G_Z, False, lambda: v_silu(14, 0), lambda: evac(15, 1), lambda: v_back(14))
            a_slice(G_Z + 4, G_Z, False, lambda: v_silu(15, 1), lambda: z_evac(0, 0), lambda: v_back(15))
            for z in (2, 3):
                a_slice(G_Z + 4 * z, G_Z, False, None, lambda: z_evac(z - 1, 1 - z % 2), None)

            def kk_evac(z):
                act.wait_ge(kk_done, z - 3)
                act.wait_ge(kk_out, 64 * (z - 4))
                blocks = pst[:, :, :].rearrange("p b (t m) -> p b t m", t=TT)
                for q in range(4):
                    r = slice(32 * q, 32 * q + 32)
                    av(kks[r, :, :, :], blocks[r, :, :, r], ACT.Copy).then_inc(kk_ev, 1)
            with act.Fori(2, 4) as i:
                for s in range(2):
                    z = 2 * i + s
                    a_slice(G_Z + 4 * z, G_Z, False, None, lambda: z_evac(z - 1, 1 - s), lambda: kk_evac(z))
            z_evac(7, 1)

            pr = Tally(c_s)
            bt1 = bt[:, 1].rearrange("p a b -> p (a b)")
            act.wait_ge(c_v, 3)
            pr.inc(av(bt1, bt[:, 0].rearrange("p a b -> p (a b)"), ACT.Abs))
            pr.wait(act)
            pr.inc(av(bt1, bt1, ACT.Exp, scale=-1.0))
            pr.wait(act)
            pr.inc(av(bt1, bt1, ACT.Ln, bias=epsr[:, 2:3]))
            pr.inc(av(alog[:, 0, :], alog[:, 0, :], ACT.Exp))
            act.wait_ge(c_v, 4)
            for t in range(TT):
                pr.inc(av(beta[:, t].rearrange("p (d v) h -> p d v h", d=2),
                          bt[:, 2, t, 0:64].rearrange("p (d h v) -> p d v h", d=2, v=2), ACT.Exp))
            act.wait_ge(c_v, C_SUB)
            sflat = sdec[:, :, :, :].rearrange("p c i j -> p (c i j)")
            pr.inc(av(sflat, sflat, ACT.Exp))
            assert pr.n == 7

            act.wait_ge(c_init, C_POOL_INV + 2)

            def step(h, par, M=True, A=True, B=True, C=True):
                b = h - 1

                def first_half(o):
                    act.wait_ge(y_done, 2 * b + o + 1)
                    for d in range(2):
                        q = slice(0, 64) if d == 0 else slice(64, P)
                        av(yh[q, 2 * d:2 * d + 2, :], ps_a[q, 2 * d:2 * d + 2, :], ACT.Copy).then_inc(yc_done, 1)

                def solution(o):
                    act.wait_ge(u_done, 2 * b + o + 1)
                    av(uu[:, o, :, :], ps_a, ACT.Copy).then_inc(uc_done, 1)

                def decays(kind, done):
                    for c in range(4):
                        i = av(dec[:, 1 - par, c, kind].rearrange("p s m -> p (s m)"),
                               exb[:, c, kind].rearrange("p s m -> p (s m)"), ACT.Exp)
                    i.then_inc(done, 1)

                if B:
                    first_half(0)
                if C:
                    act.wait_ge(o_done, h - 1)
                    act.wait_ge(oms_done, h - 2)
                    av(osq[:, :, :], ps_o, ACT.Square).then_inc(osq_done, 1)
                if B:
                    solution(0)
                if A:
                    for d in range(2):
                        act.wait_ge(w_done, 2 * h + d + 1)
                        av(wt[:, 2 * d:2 * d + 2].rearrange("p c t m -> p (c t) m"), ps_w[:, 4 * d:4 * d + 4], ACT.Copy
                           ).then_inc(wt_done, 1)
                if B:
                    first_half(1)
                if C:
                    act.wait_ge(oms_done, h - 1)
                    act.wait_ge(on_done, h - 2)
                    av(oms[:, 1, :], oms[:, 0, :], ACT.Ln, bias=epsr[:, 1:2], scale=1.0 / P).then_inc(oln_done, 1)
                    act.wait_ge(oln_done, h - 1)
                    av(oms[:, 2, :], oms[:, 1, :], ACT.Exp, scale=-0.5).then_inc(ors_done, 1)
                if B:
                    solution(1)
                if M:
                    act.wait_ge(ex_done, h + 2)
                    if B:
                        act.wait_ge(h_done, 2 * b + 2)
                    decays(0, d0_done)
                if C:
                    act.wait_ge(ot_done, h - 1)
                    av(oT[:, ds(2 * h - 4, 2), :], ps_oT, ACT.Copy).then_inc(oT_done, 1)
                if M:
                    if B:
                        act.wait_ge(o_done, b + 1)
                    decays(1, d1_done)
            step(-1, 1, A=False, B=False, C=False)
            step(0, 0, B=False, C=False)
            step(1, 1, C=False)
            with act.Fori(1, HQ // 2 - 1) as i:
                for s in range(2):
                    step(2 * i + s, s)
            step(HQ - 2, 0)
            step(HQ - 1, 1, M=False)
            step(HQ, 0, M=False, A=False)
            step(HQ + 1, 1, M=False, A=False, B=False)

            hi(G_GO, G_GO)
            hi(G_GO + 1, G_GO + 1)
            act.wait_ge(oT_done, HQ)
            for q in range(8):
                av(o_hi[:, 4 * q:4 * q + 4, :], oT[:, 4 * q:4 * q + 4, :], ACT.Copy).then_inc(osp_hi, 1)

            def y_evac(n):
                act.wait_ge(w_used, G_GO + 8 * n + 8)
                av(yg[:, :, n * NSL:(n + 1) * NSL], psg[:, (S_GO + n) % 2, :, :], ACT.Copy).then_inc(ps_read, 1)
            for j in range(2, 8):
                hi(G_GO + j, G_GO + j)
            act.wait_ge(osp_lo, 1)
            for n in range(1, 4):
                for j in range(8):
                    hi(G_GO + 8 * n + j, G_GO + j)
                    if j == 1:
                        y_evac(n - 1)
                    if j == 4:
                        out_squares(0, n - 1, yg, dump0[:, :], (ps_read, S_GO + n))
            hi(G_F0, G_F0)
            y_evac(3)
            out_squares(0, 3, yg, dump0[:, :], (ps_read, S_F0))
            hi(G_F0 + 1, G_F0 + 1)
            out_root(0)
            squares(1, lambda t: (x_up, t + 1))
            pre(1, h_hi3, hf3, 4)

            def ffn(f, g0, s0):
                nm = GRP * f

                def gate(S, par, g_end):
                    act.wait_ge(w_used, g_end)
                    act.wait_ge(ps_read, S)
                    av(sg[:, :, :], psg[:, (s0 + par) % 2], ACT.Silu).then_inc(ps_read, 1)

                def g_high(n):
                    act.wait_ge(g_tr, nm + n + 1)
                    av(g_hi[:, :, :], pst[:, :, :], ACT.Copy).then_inc(g_hi_ok, 1)
                for j in range(8):
                    if j == 5:
                        gate(s0, 0, g0 + 4)
                    if j >= 2:
                        hi(g0 + j, g0 + j)
                with act.Fori(0, (GRP - 1) // 2) as i:
                    for s in range(2):
                        n = 2 * i + s + 1
                        S, g = s0 + 2 + 12 * i + 6 * s, g0 + 8 + 24 * i + 12 * s
                        for j in range(12):
                            if j == 5:
                                gate(S, 0, g + 4)
                            hi(g + j, g0 + j)
                            if j == 2:
                                g_high(n - 1)
                gl = g0 + 8 + 12 * (GRP - 1)
                hi(gl, g0)
                hi(gl + 1, g0 + 1)
                g_high(GRP - 1)
                hi(gl + 2, g0 + 2)
                hi(gl + 3, g0 + 3)
                S = s0 + 2 + 6 * (GRP - 1)
                for j in range(4):
                    out_squares(2 * f + 1, j, y, sg[:, 0, :], (ps_read, S + j + 1))
                    if f == 0 and j == 1:
                        hi(G_P1, G_P1)
                if f == 0:
                    hi(G_P1 + 1, G_P1 + 1)
                out_root(2 * f + 1)

            ffn(0, G_F0, S_F0)
            squares(2, lambda t: (x_up, 3 + t))
            pre(2, h_hi3, hf3, 8)

            def half(n, which):
                act.wait_ge(w_used, G_P1 + 8 * n + 4 * which + 4)
                act.wait_ge(ps_read, S_P1 + 2 * n + which)
                act.wait_ge((t_a, t_g)[which], n)
                av(ev4[:, which, :, :], psg[:, (S_P1 + which) % 2], ACT.Copy).then_inc(ps_read, 1)

            def sigm(n):
                act.wait_ge(t_g, n + 1)
                act.wait_ge(glu_ok, n)
                for b in range(4):
                    i = av(sg4[:, b, :], psn[:, b, :], ACT.Sigmoid, bias=vec[:, ds(V_PW1B + KC + 4 * n + b, 1)])
                i.then_inc(sg_ok, 1)

            def products(n, part):
                act.wait_ge(glu_ok, n + 1)
                for m in part:
                    k = TAPS_S[m]
                    off = k - CTAPS // 2
                    a, e = max(0, -off), T - max(0, off)
                    act.wait_ge(dwa_ok, (len(TAPS_S) + 1) * n + max(0, m - 2))
                    for b in range(4):
                        i = av(dwp[:, m % 4, b, a:e], glu[:, b, a + off:e + off], ACT.Copy,
                               scale=vec[:, ds(NV_DW + k * KC + 4 * n + b, 1)])
                    i.then_inc(dwp_ok, 1)

            def pw1_pair(n, lag):
                for j in range(8):
                    if lag and j == 1:
                        half(n - 1, 1)
                    if j == 5:
                        half(n, 0)
                    if lag or j >= 2:
                        hi(G_P1 + 8 * n + j, G_P1 + j)
                    if lag and j == 2:
                        sigm(n - 1)
                    if lag and j >= 2:
                        products(n - 1, range(2 * j - 4, 2 * j - 2))
            pw1_pair(0, False)
            with act.Fori(1, 4) as i:
                pw1_pair(i, True)
            half(3, 1)
            sigm(3)
            products(3, range(len(TAPS_S)))
            hi(G_P2, G_P2)
            hi(G_P2 + 1, G_P2 + 1)
            for q in range(4):
                act.wait_ge(ln_v, 2 + q)
                if q >= 2:
                    act.wait_ge(ln_p, q)
                av(hf3[:, q % 2], dwo[:, 4 * q:4 * q + 4, :], ACT.Square).then_inc(ln_s, 1)
            act.wait_ge(ln_v, 6)
            av(lnst[:, 1, :], lnst[:, 1, :], ACT.Sqrt).then_inc(ln_s, 1)
            for q in range(4):
                act.wait_ge(ln_v, 8 + q)
                if q >= 2:
                    act.wait_ge(pre_lo, 12 + q - 1)
                for j in range(4):
                    kc = 4 * q + j
                    i = av(hf3[:, q % 2, j, :], dwo[:, kc, :], ACT.Silu, bias=vec[:, V_LNB + kc:V_LNB + kc + 1],
                           scale=vec[:, V_LNW + kc:V_LNW + kc + 1])
                i.then_inc(ln_s, 1)
                act.wait_ge(ln_s, 6 + 2 * q)
                av(h_hi3[:, 4 * q:4 * q + 4, :], hf3[:, q % 2], ACT.Copy).then_inc(ln_s, 1)
            for j in range(2, 4):
                hi(G_P2 + j, G_P2 + j)
            for n in range(1, 4):
                for j in range(4):
                    hi(G_P2 + 4 * n + j, G_P2 + j)
                out_squares(2, n - 1, y, sg4[:, 0:2, :].rearrange("p a t -> p (a t)"), (ps_read, S_P2 + n))
            hi(G_F1, G_F1)
            out_squares(2, 3, y, sg4[:, 0:2, :].rearrange("p a t -> p (a t)"), (ps_read, S_F1))
            hi(G_F1 + 1, G_F1 + 1)
            out_root(2)
            squares(3, lambda t: (x_up, 5 + t))
            pre(3, h_hi3, hf3, 16)
            ffn(1, G_F1, S_F1)

        @block.gpsimd
        def _(pool):
            ms, sel = nc.gpsimd.memset, nc.gpsimd.affine_select
            ms(stage[:, :, :], 0.0).then_inc(init, 1)
            ms(ones[:, :], 1.0).then_inc(init, 1)
            ms(ident[:, :], 0.0).then_inc(init, 1)
            pool.wait_ge(init, 3)
            sel(out=ident[:, :], in_=ident[:, :], compare_op=ALU.not_equal, fill=1.0, base=0,
                pattern=[[-1, P]], channel_multiplier=1).then_inc(init, 1)
            for n, e in enumerate((L2_EPS, RMS_EPS, 1.0)):
                ms(epsr[:, n:n + 1], e).then_inc(init, 1)
            pool.wait_ge(ps_read, 1)
            pool.dma_start(d_ba.rearrange("t p n -> p t n"), ba[:, :, :]).then_inc(ba_out, 16)
            with pool.Fori(0, 8) as s:
                pool.wait_ge(rn_done, s + 1)
                pool.wait_ge(kn_out, 16 * s)
                nc.gpsimd.tensor_tensor(kn[:, :, :], sv[:, :, :], rn[:, :, :], MUL).then_inc(kn_ready, 1)
                pool.wait_ge(kn_ready, s + 1)
                pool.dma_start(d_qkn[ds(4 * s, 4)].rearrange("b p t -> p b t"), kn[:, :, :]).then_inc(kn_out, 16)

            def store_v(s):
                pool.wait_ge(vb_ev, s + 1)
                pool.dma_start(d_v[:, :, ds(s * NSL, NSL)].rearrange("t p n -> p t n"),
                               kn[:, :, :].rearrange("p (t a) b -> p t (a b)", t=TT)).then_inc(kn_out, 16)

            def store_z(z, par):
                pool.wait_ge(ps_read, S_Z + z + 1)
                pool.wait_ge(z_out, 16 * z)
                for t in range(TT):
                    i = nc.gpsimd.tensor_tensor(zw[:, t, :].rearrange("p (a b) -> p a b", b=P),
                                                ev[:, par, t, :].rearrange("p (a b) -> p a b", b=P), gwb[:, :, :], MUL)
                i.then_inc(zw_done, 1)
                pool.wait_ge(zw_done, z + 1)
                pool.dma_start(d_z[:, :, ds(z * NSL, NSL)].rearrange("t p n -> p t n"), zw[:, :, :]).then_inc(z_out, 16)
            with pool.Fori(0, 7) as s:
                store_v(s)
            pool.wait_ge(gw_land, 64)
            store_z(0, 0)
            store_v(7)
            store_z(1, 1)
            store_z(2, 0)
            pool.wait_ge(kn_out, 16 * 16)
            with pool.Fori(2, 4) as i:
                for s in range(2):
                    z = 2 * i + s
                    pool.wait_ge(kk_done, z - 4)
                    pool.dma_start(kst[:, :, :], d_qkn[ds(HQ + 4 * z - 16, 4)].rearrange("b p t -> p b t")).then_inc(kst_land, 16)
                    store_z(z - 1, 1 - s)
                    pool.wait_ge(kk_ev, 4 * (z - 3))
                    dst = d_kk[ds((4 * z - 16) * NBLK, 4 * NBLK)].rearrange("(h t q) i j -> q i h t j", t=TT, q=4)
                    for q in range(4):
                        pool.dma_start(dst[q], kks[32 * q:32 * q + 32, :, :, :]).then_inc(kk_out, 16)
            store_z(7, 1)

            def cw(n, dst, ready):
                pool.wait_ge(cwc_ok, n + 1)
                pool.dma_start(d_cw[n].rearrange("(k p) -> p k", p=P), cwc[:, n, :],
                               allow_slow_non_contiguous=True).then_inc(cw_out, 16)
                pool.wait_ge(cw_out, 16 * (n + 1))
                pool.wait_ge(*ready)
                pool.dma_start(dst[:, :], d_cw[n].partition_broadcast(P)).then_inc(cw_land, 16)

            pr = Tally(c_init)
            pool.wait_ge(c_land, 64)
            for kind, value in ((0, -1.0), (1, float(P) ** -0.5)):
                pr.inc(ms(masks[:, :, kind], value))
            pr.wait(pool)
            for d in range(2):
                for kind in range(2):
                    for seg in (0, 2):
                        m, sign = masks[:, d, kind, seg, :], 1 - 2 * d
                        pr.inc(sel(out=m, in_=m, compare_op=ALU.is_gt if kind == 0 else ALU.is_ge, fill=0.0, base=0,
                                   pattern=[[sign, P]], channel_multiplier=-sign))
            pr.inc(ms(tri[:, :, :], 1.0))
            pr.wait(pool)
            for n, (sign, op) in enumerate(((1, ALU.is_ge), (-1, ALU.is_gt), (-1, ALU.is_ge), (1, ALU.is_gt))):
                pr.inc(sel(out=tri[:, n, :], in_=tri[:, n, :], compare_op=op, fill=0.0, base=0,
                           pattern=[[sign, P]], channel_multiplier=-sign))
            pr.inc(ms(m64[:, :, :], 0.0))
            pr.wait(pool)
            for d in range(2):
                for b in (0, 64):
                    r = b + 32 * d
                    pr.inc(ms(m64[r:r + 32, d, b + 32 - 32 * d:b + 64 - 32 * d], 1.0))
                    pr.wait(pool)
            pr.inc(ms(sinv[:, 0], 0.0))
            pr.wait(pool)
            pr.inc(ms(sinv[:, 0].rearrange("p c i j -> p c (i j)")[:, :, 0:1024:33], 1.0))
            assert pr.n == C_POOL
            pool.wait_ge(c_v, C_DEC)
            invert(pool, nc.gpsimd, pr, ((1, 1, 2),))
            assert pr.n == C_POOL_INV
            pool.wait_ge(inv_out, 16)
            pr.inc(ms(inv[:, :, :, :, :], 0.0))
            pr.inc(ms(yh[:, :, :], 0.0))


            def step(h, par, A=True, C=True):
                if A:
                    pool.wait_ge(mk_done, h + 1)
                    pool.wait_ge(d1_done, h + 1)
                    for c in range(4):
                        f = dec[:, par, c, 1].rearrange("p s m -> p (s m)")
                        i = nc.gpsimd.tensor_tensor(f, f, mk[:, c // 2, 1].rearrange("p s m -> p (s m)"), MUL)
                    i.then_inc(aq_done, 1)
                    pool.wait_ge(v_land, 16 * (h + 1))
                    if not isinstance(h, int) or h > 1:
                        pool.wait_ge(uc_done, 2 * h - 2)
                    for o in range(2):
                        for d in range(2):
                            t = o if d == 0 else 1 - o
                            nc.gpsimd.tensor_tensor(rv[:, par, o, 2 * d:2 * d + 2, :], vt[:, t, :, :],
                                                    beta[:, t, 2 * d:2 * d + 2, ds(h, 1)].broadcast_to([P, 2, P]),
                                                    MUL).then_inc(rv_done, 1)
                if C:
                    pool.wait_ge(on_done, h - 1)
                    pool.wait_ge(z_land, 16 * (h - 1))
                    nc.gpsimd.tensor_tensor(og[:, :, :], og[:, :, :], zt[:, :, :, :].rearrange("p t a m -> p (t a) m"),
                                            MUL).then_inc(og_done, 1)
            step(0, 0, C=False)
            step(1, 1, C=False)
            with pool.Fori(1, HQ // 2) as i:
                for s in range(2):
                    step(2 * i + s, s)
            step(HQ, 0, A=False)
            step(HQ + 1, 1, A=False)
            cw(0, cwb0, (oT_done, HQ))
            cw(1, cwb, (x_up, 2))
            one = ones[:, 0:1].unsqueeze(2).broadcast_to([P, 4, T])
            with pool.Fori(0, 4) as n:
                steps = (len(TAPS_S) + 1) * n
                pool.wait_ge(dw_ok, n)
                pool.wait_ge(x_up, 4)
                nc.gpsimd.tensor_tensor(dwa, one, one, SUB).then_inc(dwa_ok, 1)
                for m, k in enumerate(TAPS_S):
                    off = k - CTAPS // 2
                    a, e = max(0, -off), T - max(0, off)
                    pool.wait_ge(dwp_ok, len(TAPS_S) * n + m + 1)
                    pool.wait_ge(dwa_ok, steps + m + 1)
                    nc.gpsimd.tensor_tensor(dwa[:, :, a:e], dwa[:, :, a:e], dwp[:, m % 4, :, a:e], ADD).then_inc(dwa_ok, 1)
            cw(2, cwb, (x_up, 4))
            cw(3, cwb, (x_up, 6))


_INS = ["x", "c", "ada_w", "ada_b", "norm_w", "gdn_in_w", "gdn_conv_w", "gdn_A_log", "gdn_dt_bias", "gdn_norm_w",
        "gdn_out_w", "cf_pw1_w", "cf_pw1_b", "cf_dw_w", "cf_dw_b", "cf_ln_w", "cf_ln_b", "cf_pw2_w", "cf_pw2_b",
        "ffn_in_w", "ffn_out_w"]


def kernel(**inputs):
    import numpy as np
    import concourse.bacc as bacc
    from concourse.bass_utils import run_bass_kernel_spmd

    nc = bacc.Bacc("TRN2", target_bir_lowering=False, num_devices=1)
    arrays, args = {}, []
    for name in _INS:
        a = np.ascontiguousarray(inputs[name])
        arrays["in_" + name] = a
        args.append(nc.dram_tensor("in_" + name, a.shape, mybir.dt.from_np(a.dtype), kind="ExternalInput").ap())
    shape = tuple(inputs["x"].shape)
    args.append(nc.dram_tensor("out_x", shape, mybir.dt.float32, kind="ExternalOutput").ap())
    build(nc, *args)
    r = run_bass_kernel_spmd(nc, [arrays], core_ids=[0])
    return r.results[0]["out_x"]
```
